# Optimizing a Trainium2 kernel written in Bass

```python
import math
import jax, jax.numpy as jnp
from jax import lax
import numpy as np

D_MODEL = 1024
BATCH = 1
SEQ = 1024
DEPTH = 1

GMLP_WIDTH = D_MODEL
GMLP_GROUPS = 8
GMLP_GROUP_DIM = GMLP_WIDTH // GMLP_GROUPS
GMLP_CHUNK = 128
HGRN_HEADS = 8
HGRN_DK = 128
HGRN_DV = D_MODEL // HGRN_HEADS
HGRN_KEY_WIDTH = HGRN_HEADS * HGRN_DK
HGRN_VAL_WIDTH = HGRN_HEADS * HGRN_DV
HGRN_CHUNK = 64
HGRN_SCALE = HGRN_DK ** -0.5
N_BRANCHES = 2
D_FF = -(-(8 * D_MODEL) // (3 * 256)) * 256
IN_SIZES = (GMLP_WIDTH, GMLP_WIDTH, HGRN_KEY_WIDTH, HGRN_KEY_WIDTH,
            HGRN_VAL_WIDTH, HGRN_VAL_WIDTH, D_MODEL, D_MODEL)
IN_WIDTH = sum(IN_SIZES)
NORM_EPS = 1e-6

kernel_name = "gmlp_hgrn2_gated_hybrid_block"

def _split_points(sizes):
    pts, acc = [], 0
    for s in sizes[:-1]:
        acc += s
        pts.append(acc)
    return pts

def rms_norm(x, gain):
    xf = x.astype(jnp.float32)
    y = xf * lax.rsqrt(jnp.mean(xf * xf, axis=-1, keepdims=True) + NORM_EPS)
    return (y * gain.astype(jnp.float32)).astype(x.dtype)

def layer_norm(x, gain, bias):
    xf = x.astype(jnp.float32)
    mu = jnp.mean(xf, axis=-1, keepdims=True)
    var = jnp.mean(jnp.square(xf - mu), axis=-1, keepdims=True)
    y = (xf - mu) * lax.rsqrt(var + NORM_EPS)
    return (y * gain.astype(jnp.float32) + bias.astype(jnp.float32)).astype(x.dtype)

def gmlp_spatial_gating(u, v, ln_g, ln_b, w_s, b_s):
    B, S, _ = v.shape
    n_chunks = S // GMLP_CHUNK
    v = layer_norm(v, ln_g, ln_b)
    vc = v.reshape(B, n_chunks, GMLP_CHUNK, GMLP_GROUPS, GMLP_GROUP_DIM)
    causal = jnp.tril(jnp.ones((GMLP_CHUNK, GMLP_CHUNK), dtype=bool))
    w = jnp.where(causal, w_s, jnp.zeros((), w_s.dtype)).astype(v.dtype)
    mixed = jnp.einsum('gts,bnsgd->bntgd', w, vc) + b_s.T.astype(v.dtype)[:, :, None]
    return u * mixed.reshape(B, S, GMLP_WIDTH)

def hgrn2_chunkwise(q, f_logit, v, lb):
    B, S, _ = q.shape
    C = HGRN_CHUNK
    n_chunks = S // C
    f32 = jnp.float32
    lb = lb.astype(f32)
    f = lb + (1.0 - lb) * jax.nn.sigmoid(f_logit.astype(f32))
    k = 1.0 - f
    log_f = jnp.log(f)

    def to_chunks(t, d):
        return t.reshape(B, n_chunks, C, HGRN_HEADS, d).transpose(0, 3, 1, 2, 4)

    qc = to_chunks(q.astype(f32), HGRN_DK) * HGRN_SCALE
    kc = to_chunks(k, HGRN_DK)
    vc = to_chunks(v.astype(f32), HGRN_DV)
    A = jnp.cumsum(to_chunks(log_f, HGRN_DK), axis=3)
    A_mid = A[:, :, :, C // 2 - 1:C // 2, :]
    A_last = A[:, :, :, C - 1:C, :]

    q_in = qc * jnp.exp(A - A_mid)
    k_in = kc * jnp.exp(A_mid - A)
    causal = jnp.tril(jnp.ones((C, C), dtype=bool))
    scores = jnp.where(causal, jnp.einsum('bhctk,bhcsk->bhcts', q_in, k_in), 0.0)
    o_intra = jnp.einsum('bhcts,bhcsv->bhctv', scores, vc)

    dS = jnp.einsum('bhcsk,bhcsv->bhckv', kc * jnp.exp(A_last - A), vc)
    decay = jnp.exp(A_last[:, :, :, 0, :])

    def step(S_prev, xs):
        d, ds = xs
        return d[..., None] * S_prev + ds, S_prev

    S0 = jnp.zeros((B, HGRN_HEADS, HGRN_DK, HGRN_DV), f32)
    _, S_before = lax.scan(step, S0, (jnp.moveaxis(decay, 2, 0), jnp.moveaxis(dS, 2, 0)))
    S_before = jnp.moveaxis(S_before, 0, 2)
    o_inter = jnp.einsum('bhctk,bhckv->bhctv', qc * jnp.exp(A), S_before)

    o = o_intra + o_inter
    return o.transpose(0, 2, 3, 1, 4).reshape(B, S, HGRN_HEADS, HGRN_DV)

def setup_inputs(seed: int = 0) -> dict:
    key = jax.random.key(seed)
    ks = jax.random.split(key, 16)
    f32 = jnp.float32

    def normal(k, shape, scale):
        return jax.random.normal(k, shape, f32) * scale

    return {
        "x": normal(ks[0], (BATCH, SEQ, D_MODEL), 1.0),
        "norm_mix_g": 1.0 + normal(ks[1], (DEPTH, D_MODEL), 0.05),
        "w_in": normal(ks[2], (DEPTH, D_MODEL, IN_WIDTH), D_MODEL ** -0.5),
        "gmlp_ln_g": 1.0 + normal(ks[3], (DEPTH, GMLP_WIDTH), 0.05),
        "gmlp_ln_b": normal(ks[4], (DEPTH, GMLP_WIDTH), 0.02),
        "gmlp_w_s": normal(ks[5], (DEPTH, GMLP_GROUPS, GMLP_CHUNK, GMLP_CHUNK), GMLP_CHUNK ** -0.5),
        "gmlp_b_s": 1.0 + normal(ks[6], (DEPTH, GMLP_GROUPS, GMLP_CHUNK), 0.1),
        "hgrn_lb_table": normal(ks[7], (DEPTH + 1, HGRN_KEY_WIDTH), 0.5),
        "hgrn_norm_g": 1.0 + normal(ks[8], (DEPTH, HGRN_DV * HGRN_HEADS), 0.05),
        "w_branch_a": normal(ks[9], (DEPTH, GMLP_WIDTH, D_MODEL), GMLP_WIDTH ** -0.5),
        "w_branch_b": normal(ks[10], (DEPTH, HGRN_VAL_WIDTH, D_MODEL), HGRN_VAL_WIDTH ** -0.5),
        "w_out": normal(ks[11], (DEPTH, D_MODEL, D_MODEL), D_MODEL ** -0.5),
        "norm_ffn_g": 1.0 + normal(ks[12], (DEPTH, D_MODEL), 0.05),
        "w_gate_up": normal(ks[13], (DEPTH, D_MODEL, 2 * D_FF), D_MODEL ** -0.5),
        "w_down": normal(ks[14], (DEPTH, D_FF, D_MODEL), D_FF ** -0.5),
        "norm_final_g": 1.0 + normal(ks[15], (D_MODEL,), 0.05),
    }

def reference(x, norm_mix_g, w_in, gmlp_ln_g, gmlp_ln_b, gmlp_w_s, gmlp_b_s,
              hgrn_lb_table, hgrn_norm_g, w_branch_a, w_branch_b, w_out,
              norm_ffn_g, w_gate_up, w_down, norm_final_g):
    B, S, _ = x.shape
    split_pts = _split_points(IN_SIZES)
    lb_all = jnp.cumsum(jax.nn.softmax(hgrn_lb_table.astype(jnp.float32), axis=0), axis=0)

    for l in range(DEPTH):
        h = rms_norm(x, norm_mix_g[l])
        proj = jnp.einsum('bsd,de->bse', h, w_in[l])
        u, v, q, f_logit, i_val, g_out, gate_a, gate_b = jnp.split(proj, split_pts, axis=-1)

        a = gmlp_spatial_gating(jax.nn.gelu(u), jax.nn.gelu(v), gmlp_ln_g[l], gmlp_ln_b[l],
                                gmlp_w_s[l], gmlp_b_s[l])
        y_a = jnp.einsum('bse,ed->bsd', a, w_branch_a[l])

        o = hgrn2_chunkwise(q, f_logit, i_val, lb_all[l])
        o = o * lax.rsqrt(jnp.mean(o * o, axis=-1, keepdims=True) + NORM_EPS)
        o = (o.reshape(B, S, HGRN_VAL_WIDTH) * hgrn_norm_g[l].astype(jnp.float32)).astype(x.dtype)
        o = o * jax.nn.silu(g_out)
        y_b = jnp.einsum('bse,ed->bsd', o, w_branch_b[l])

        merged = jax.nn.sigmoid(gate_a) * y_a + jax.nn.sigmoid(gate_b) * y_b
        x = x + jnp.einsum('bsd,de->bse', merged, w_out[l])

        h = rms_norm(x, norm_ffn_g[l])
        gu = jnp.einsum('bsd,df->bsf', h, w_gate_up[l])
        gate, up = jnp.split(gu, [D_FF], axis=-1)
        x = x + jnp.einsum('bsf,fd->bsd', jax.nn.silu(gate) * up, w_down[l])

    return rms_norm(x, norm_final_g)


_drawn_inputs = setup_inputs


def setup_inputs(seed=0):
    import zlib

    import numpy as np

    out = dict(_drawn_inputs(seed))
    spreads = {}
    factors = {'gmlp_ln_g': 4.974,
     'gmlp_ln_b': 24.535,
     'hgrn_norm_g': 3.755,
     'gmlp_b_s': 2.959,
     'norm_ffn_g': 2.784}
    for name, (base, spread) in spreads.items():
        noise = np.random.default_rng([zlib.crc32(name.encode()), seed]).standard_normal(out[name].shape)
        drawn = base * np.exp(spread * noise) if base else spread * noise
        out[name] = __import__('jax').numpy.asarray(drawn.astype(out[name].dtype))
    for name, factor in factors.items():
        out[name] = (out[name] * factor).astype(out[name].dtype)
    return out
```

```python
from contextlib import ExitStack

import concourse.bass as bass
from concourse import mybir

F32 = mybir.dt.float32
F32R = mybir.dt.float32r
I32 = mybir.dt.int32
ACT = mybir.ActivationFunctionType
ALU = mybir.AluOpType

P = 128
T = 1024
H = T // 2
D = 1024
KC = D // P
HEADS = 8
CH = 64
NCH = T // CH
NSC = T // P
D_FF = -(-(8 * D) // (3 * 256)) * 256
FC = D_FF // P
EPS = 1e-6
DK_SCALE = float(P) ** -0.5

PARTS = [8, 7, 7]
assert sum(PARTS) == FC

N_HEAD = 0
N_GATE_B = N_HEAD + 4 * HEADS
N_OUT_B = N_GATE_B + KC
N_V = N_OUT_B + KC
N_U = N_V + KC
N_GATE_A = N_U + KC
N_MERGE = N_GATE_A + 2 * KC
N_PART = []
_n = N_MERGE + KC
for _p in PARTS:
    N_PART.append(_n)
    _n += 2 * _p + KC
N_BLOCKS = _n

POOL_SQUARES = 3

V_MIX, V_LB0, V_LB1, V_HG, V_LNG, V_LNB, V_FFN, V_FIN = range(8)


def build(nc, x_t, w_stream, vectors, w_spatial, b_spatial, out_t):
    with ExitStack() as ctx:
        def sb(name, shape, dt=F32, stack=ctx):
            return stack.enter_context(nc.sbuf_tensor(name, shape, dt))

        def sem(name):
            return ctx.enter_context(nc.semaphore(name))

        vecs = sb("vecs", [P, 8, KC])
        lb = sb("lb", [P, KC])
        one_minus_lb = sb("one_minus_lb", [P, KC])
        lb_tmp = sb("lb_tmp", [P, 4, KC])
        ones = sb("ones", [P, P])
        ident = sb("ident", [P, P])
        causal = sb("causal", [P, P])
        dec = sb("dec", [P, NCH])
        dec2 = sb("dec2", [P, NSC])
        inv_rms = sb("inv_rms", [P, T])
        stats = sb("stats", [P, NSC, 2, 6])
        mean_var = sb("mean_var", [P, NSC, 2])
        ln_ve = sb("ln_ve", [P, NSC])
        ln_r = sb("ln_r", [P, NSC])
        ln_t = sb("ln_t", [P, NSC])
        spatial_t = sb("spatial_t", [P, KC, P])
        w_raw = [sb(f"w_raw{i}", [P, KC, P]) for i in range(2)]
        w_hi = [sb(f"w_hi{i}", [P, KC, P], F32R) for i in range(2)]
        w_lo = [sb(f"w_lo{i}", [P, KC, P], F32R) for i in range(2)]
        h_hi = sb("h_hi", [P, KC, T], F32R)
        h_lo = sb("h_lo", [P, KC, T], F32R)

        def alias(name, shape, dt=F32):
            with nc.sbuf_tensor(name, shape, dt) as t:
                return t
        x_in = alias("x_in", [P, KC, T])
        o_raw = alias("o_raw", [P, KC, T])
        o_lo = alias("o_lo", [P, KC, T], F32R)
        v_tok = alias("v_tok", [P, KC, NSC, P])
        a_hi = alias("a_hi", [P, KC, T], F32R)
        resid = sb("resid", [P, KC, T])
        work = [sb(f"work{i}", [P, T]) for i in range(3)]
        q_sc, s_gate, o_sq = work
        with ExitStack() as heads:
            def hb(name, shape=(P, T)):
                return sb(name, list(shape), F32, heads)
            fgt, key, cum, to_last = hb("fgt"), hb("key"), hb("cum"), hb("to_last")
            k_mid, q_mid, k_out, k_tok = hb("k_mid"), hb("q_mid"), hb("k_out"), hb("k_tok")
            k_end, q_cum, i_feat, i_tok = hb("k_end"), hb("q_cum"), hb("i_feat"), hb("i_tok")
            qry, keep = hb("qry"), hb("keep")
            scores = hb("scores", (P, NSC, P))
            state = hb("state", (P, NSC, P))
        merged = alias("merged", [P, KC, T])
        merged_lo = alias("merged_lo", [P, KC, T], F32R)
        squares = alias("squares", [P, KC, T])
        act_lo = sb("act_lo", [P, KC, T], F32R)
        act_hi = h_hi
        o_hi = alias("o_hi", [P, KC, T], F32R)
        a_lo = alias("a_lo", [P, KC, T], F32R)
        with ExitStack() as late:
            sb("_a_lo_0_to_4", [P, 5, T], F32, late)
            b_bcast = sb("b_bcast", [P, KC, P], F32, late)
            sb("_a_lo_6", [P, T], F32, late)
            mix_bias = sb("mix_bias", [P, KC, P], F32, late)
        ffn_hi = sb("ffn_hi", [P, KC, T], F32R)

        proj = [ctx.enter_context(nc.psum_tensor(f"proj{i}", [P, T], F32)) for i in range(2)]
        ps_a = ctx.enter_context(nc.psum_tensor("ps_a", [P, T], F32))
        ps_b = ctx.enter_context(nc.psum_tensor("ps_b", [P, T], F32))

        w_loaded = [sem(f"w_loaded{i}") for i in range(2)]
        w_hi_ready, w_lo_ready = sem("w_hi_ready"), sem("w_lo_ready")
        proj_done = sem("proj_done")
        x_loaded = [sem(f"x_loaded{i}") for i in range(KC)]
        x_again = [sem(f"x_again{i}") for i in range(KC)]
        vec_loaded, wsp_loaded, bsp_loaded = sem("vec_loaded"), sem("wsp_loaded"), sem("bsp_loaded")
        out_stored = sem("out_stored")
        pool_const = sem("pool_const")
        lb_exp, lb_step = sem("lb_exp"), sem("lb_step")
        const_ready, rowsum_done, bias_ready = sem("const_ready"), sem("rowsum_done"), sem("bias_ready")
        sq_ready, sq_pool, ssq_first, ssq_step, ssq_done = (
            sem("sq_ready"), sem("sq_pool"), sem("ssq_first"), sem("ssq_step"), sem("ssq_done"))
        ve_ready, r0_ready = sem("ve_ready"), sem("r0_ready")
        newton, rms_ready = sem("newton"), sem("rms_ready")
        ffn_hi_ready, ffn_lo_ready = sem("ffn_hi_ready"), sem("ffn_lo_ready")
        f_scaled, g_scaled, gb_scaled, v_scaled, u_scaled, ga_scaled, ff_scaled = (
            sem("f_scaled"), sem("g_scaled"), sem("gb_scaled"), sem("v_scaled"), sem("u_scaled"),
            sem("ga_scaled"), sem("ff_scaled"))
        h_hi_ready, h_lo_ready = sem("h_hi_ready"), sem("h_lo_ready")
        sig_ready, f_ready, key_ready, logf_ready, cum_ready = (
            sem("sig_ready"), sem("f_ready"), sem("key_ready"), sem("logf_ready"), sem("cum_ready"))
        mid_ready, last_ready = sem("mid_ready"), sem("last_ready")
        qry_ready, dec_ready, dec2_ready = sem("qry_ready"), sem("dec_ready"), sem("dec2_ready")
        exp_mid, exp_out = sem("exp_mid"), sem("exp_out")
        k_mid_ready, q_mid_ready = sem("k_mid_ready"), sem("q_mid_ready")
        k_end_ready, q_cum_ready = sem("k_end_ready"), sem("q_cum_ready")
        k_out_ready, q_sc_ready = sem("k_out_ready"), sem("q_sc_ready")
        i_feat_ready, i_tok_ready, k_tok_ready = sem("i_feat_ready"), sem("i_tok_ready"), sem("k_tok_ready")
        i_turned, k_turned = sem("i_turned"), sem("k_turned")
        ds_done, state_step = sem("ds_done"), sem("state_step")
        diag_done, cross_done, diag_ready, cross_ready = (
            sem("diag_done"), sem("cross_done"), sem("diag_ready"), sem("cross_ready"))
        o_done, osq_ready, osum_done = sem("o_done"), sem("osq_ready"), sem("osum_done")
        gate_ready, ob_ready, o_ready = sem("gate_ready"), sem("ob_ready"), sem("o_ready")
        ove_ready, or0_ready, onewton = sem("ove_ready"), sem("or0_ready"), sem("onewton")
        o_hi_ready, o_lo_ready = sem("o_hi_ready"), sem("o_lo_ready")
        gate_b_ready, part_ready = sem("gate_b_ready"), sem("part_ready")
        vg_ready, v_turned, v_tok_ready = sem("vg_ready"), sem("v_turned"), sem("v_tok_ready")
        z_centred = sem("z_centred")
        stat_step, ln_r0_ready, bn_step = sem("stat_step"), sem("ln_r0_ready"), sem("bn_step")
        ug_ready, z_ready, mixed_done = sem("ug_ready"), sem("z_ready"), sem("mixed_done")
        mix_ready, a_raw_ready, a_hi_ready, a_lo_ready = (
            sem("mix_ready"), sem("a_raw_ready"), sem("a_hi_ready"), sem("a_lo_ready"))
        gate_a_ready, ya_ready, m_ready = sem("gate_a_ready"), sem("ya_ready"), sem("m_ready")
        m_hi_ready, m_lo_ready = sem("m_hi_ready"), sem("m_lo_ready")
        x1_ready, x1_sq = sem("x1_ready"), sem("x1_sq")
        silu_scaled = sem("silu_scaled")
        silu_ready, act_raw, act_hi_ready, act_lo_ready = (
            sem("silu_ready"), sem("act_raw"), sem("act_hi_ready"), sem("act_lo_ready"))
        down_ready = sem("down_ready")
        tail_done = sem("tail_done")
        out_ready = sem("out_ready")

        block = ctx.enter_context(nc.Block())

        def f32(ap):
            return ap.bitcast(F32)

        def chunks(t2d):
            return t2d.rearrange("p (c t) -> p c t", t=CH)

        def later(k):
            return not isinstance(k, int) or k > 0

        def stepped(engine, count, body):
            body(0)
            with engine.Fori(1, count) as k:
                body(k)

        def supers(t2d):
            return t2d.rearrange("p (c t) -> p c t", t=P)

        last_parts = PARTS[-1]
        n_tail = N_PART[-1] + 2 * last_parts

        def tail_weight(c):
            if c < 2:
                return w_hi[c][:, 0:last_parts, :], w_lo[c][:, 0:last_parts, :]
            return tuple(t[:, c - 2, 0:last_parts * P].rearrange("p (k n) -> p k n", n=P) for t in (ffn_hi, h_lo))

        def tail_bank(q):
            return proj[q // 2 % 2][:, q % 2 * H:q % 2 * H + H]

        act_before = [sum(PARTS[:i]) for i in range(len(PARTS))]

        @block.sync
        def _(sp):
            sp.dma_start(vecs[:], vectors).then_inc(vec_loaded, 16)
            for c in range(KC):
                sp.dma_start(x_in[:, c, :], x_t[:, c, :]).then_inc(x_loaded[c], 16)
                if c in (0, 4):
                    sp.dma_start(w_raw[c // 4][:], w_stream[c // 4]).then_inc(w_loaded[c // 4], 16)
            with sp.Fori(1, N_BLOCKS // 2) as pair:
                for i in range(2):
                    sp.wait_ge(w_lo_ready, 2 * pair + (i - 1))
                    sp.dma_start(w_raw[i][:], w_stream[2 * pair + i]).then_inc(w_loaded[i], 16)
            for half in range(2):
                s = slice(half * H, half * H + H)
                for c in range(KC):
                    sp.wait_ge(out_ready, KC * half + c + 1)
                    sp.dma_start(out_t[:, c, s], resid[:, c, s]).then_inc(out_stored, 16)
            sp.wait_ge(out_stored, 16 * 2 * KC)

        @block.gpsimd
        def _(pool):
            nc.gpsimd.memset(ones[:], 1.0).then_inc(const_ready, 1)
            nc.gpsimd.memset(ident[:], 0.0).then_inc(pool_const, 1)
            nc.gpsimd.memset(causal[:], 1.0).then_inc(pool_const, 1)
            pool.wait_ge(pool_const, 2)
            nc.gpsimd.affine_select(out=ident[:], in_=ident[:], compare_op=ALU.not_equal, fill=1.0, base=0,
                                    pattern=[[1, P]], channel_multiplier=-1).then_inc(const_ready, 1)
            nc.gpsimd.affine_select(out=causal[:], in_=causal[:], compare_op=ALU.is_ge, fill=0.0, base=0,
                                    pattern=[[1, P]], channel_multiplier=-1).then_inc(pool_const, 1)
            pool.wait_ge(pool_const, 3)
            nc.gpsimd.memset(causal[0:CH, CH:P], 0.0).then_inc(const_ready, 1)
            for c in range(POOL_SQUARES):
                pool.wait_ge(x_loaded[c], 16)
                nc.gpsimd.tensor_tensor(squares[:, c, :], x_in[:, c, :], x_in[:, c, :], ALU.mult).then_inc(sq_pool, 1)
            for c in range(1, POOL_SQUARES):
                pool.wait_ge(sq_pool, POOL_SQUARES + c - 1)
                nc.gpsimd.tensor_tensor(squares[:, 0, :], squares[:, 0, :], squares[:, c, :], ALU.add
                                        ).then_inc(sq_pool, 1)
            pool.dma_start(spatial_t[:], w_spatial).then_inc(wsp_loaded, 16)
            pool.wait_ge(wsp_loaded, 16)
            nc.gpsimd.affine_select(out=spatial_t[:], in_=spatial_t[:], compare_op=ALU.is_ge, fill=0.0, base=0,
                                    pattern=[[0, KC], [1, P]], channel_multiplier=-1).then_inc(const_ready, 1)
            pool.wait_ge(proj_done, 2 * N_V)
            pool.dma_start(b_bcast[:].rearrange("p g t -> p (g t)"),
                           b_spatial.broadcast_to([P, KC * P])).then_inc(bsp_loaded, 16)
            pool.wait_ge(proj_done, 2 * N_MERGE)
            for c in range(KC):
                pool.dma_start(resid[:, c, :], x_t[:, c, :]).then_inc(x_again[c], 16)

        @block.scalar
        def _(act):
            def split_hi(n, i):
                act.wait_ge(w_loaded[i], 8 * (n - i) + 16)
                if not isinstance(n, int) or n >= 2:
                    act.wait_ge(proj_done, 2 * n - 2)
                nc.scalar.copy(w_hi[i][:], w_raw[i][:]).then_inc(w_hi_ready, 1)

            def rms_guess(s, count):
                act.wait_ge(ve_ready, count)
                nc.scalar.activation(inv_rms[:, s], work[0][:, s], ACT.Abs_reciprocal_sqrt).then_inc(r0_ready, 1)

            act.wait_ge(vec_loaded, 16)
            for c in range(KC):
                act.wait_ge(x_loaded[c], 16)
                nc.scalar.activation(h_hi[:, c, :], x_in[:, c, :], ACT.Copy,
                                     scale=vecs[:, V_MIX, c:c + 1]).then_inc(h_hi_ready, 1)
                if c == 0:
                    split_hi(0, 0)
            split_hi(1, 1)
            for c in range(POOL_SQUARES, KC):
                nc.scalar.activation(squares[:, c, :], x_in[:, c, :], ACT.Square).then_inc(sq_ready, 1)
            act.wait_ge(lb_step, 3)
            nc.scalar.activation(lb_tmp[:, 1:3, :], lb_tmp[:, 1:3, :], ACT.Exp).then_inc(lb_exp, 1)
            rms_guess(slice(0, T), 1)

            def gate_b(c):
                act.wait_ge(gb_scaled, c + 1)
                nc.scalar.activation(merged[:, c, :], merged[:, c, :], ACT.Sigmoid).then_inc(gate_b_ready, 1)

            def head(h, own=True):
                n = 4 * h
                small = later(h)
                if later(h):
                    split_hi(n + 1, 1)
                split_hi(n + 2, 0)
                if own:
                    act.wait_ge(f_scaled, h + 1)
                    nc.scalar.activation(fgt[:], fgt[:], ACT.Sigmoid).then_inc(sig_ready, 1)
                    act.wait_ge(key_ready, h + 1)
                    nc.scalar.activation(fgt[:], fgt[:], ACT.Ln).then_inc(logf_ready, 1)
                else:
                    gate_b(0)
                if own:
                    act.wait_ge(last_ready, h + 1)
                    if small:
                        act.wait_ge(q_sc_ready, 2 * h)
                    nc.scalar.activation(dec[:], chunks(cum[:])[:, :, CH - 1], ACT.Exp).then_inc(dec_ready, 1)
                    if small:
                        act.wait_ge(diag_done, h)
                    nc.scalar.activation(k_mid[:], fgt[:], ACT.Exp, scale=-1.0).then_inc(exp_mid, 1)
                    nc.scalar.activation(q_mid[:], fgt[:], ACT.Exp).then_inc(exp_mid, 1)
                else:
                    gate_b(1)
                split_hi(n + 3, 1)
                if own:
                    if small:
                        act.wait_ge(cross_done, h)
                        act.wait_ge(k_out_ready, 2 * h)
                    nc.scalar.activation(k_end[:], to_last[:], ACT.Exp).then_inc(exp_out, 1)
                    nc.scalar.activation(q_cum[:], cum[:], ACT.Exp).then_inc(exp_out, 1)
                else:
                    gate_b(2)
                if small:
                    act.wait_ge(o_done, h)
                    if not isinstance(h, int) or h >= 2:
                        act.wait_ge(o_ready, h - 1)
                    nc.scalar.activation(o_sq[:], ps_b[:], ACT.Square).then_inc(osq_ready, 1)
                split_hi(n + 4, 0)
                if small:
                    act.wait_ge(ove_ready, h)
                    nc.scalar.activation(k_tok[:], o_sq[:], ACT.Abs_reciprocal_sqrt).then_inc(or0_ready, 1)
                if own:
                    act.wait_ge(g_scaled, h + 1)
                    nc.scalar.activation(s_gate[:], s_gate[:], ACT.Silu).then_inc(gate_ready, 1)
                else:
                    gate_b(3)

            head(0)
            head(1)
            with act.Fori(2, HEADS) as h:
                head(h)
            act.wait_ge(q_sc_ready, 2 * HEADS)
            head(HEADS, own=False)

            act.wait_ge(o_ready, HEADS)
            for k in range(4):
                split_hi(N_GATE_B + 5 + k, 1 - k % 2)
                for j in range(2):
                    nc.scalar.copy(o_hi[:, 2 * k + j, :], o_raw[:, 2 * k + j, :]).then_inc(o_hi_ready, 1)
                gate_b(4 + k)
            with act.Fori(0, KC // 2) as k:
                for i in range(2):
                    split_hi(2 * k + (N_OUT_B + 1 + i), 1 - i)

            def v_pair(k):
                for i in range(2):
                    split_hi(2 * k + (N_V + 1 + i), 1 - i)
                    act.wait_ge(v_scaled, 2 * k + (i + 1))
                    nc.scalar.activation(work[i][:], work[i][:], ACT.Gelu_apprx_tanh).then_inc(vg_ready, 1)
            stepped(act, KC // 2, v_pair)

            def copy_a(g):
                act.wait_ge(a_raw_ready, g + 1)
                nc.scalar.copy(a_hi[:, g, :], work[1][:]).then_inc(a_hi_ready, 1)

            def u_pair(k):
                for i in range(2):
                    g = 2 * k + i
                    split_hi(g + (N_U + 1), 1 - i)
                    if i or later(k):
                        copy_a(g - 1)
                    else:
                        act.wait_ge(stat_step, 1)
                        nc.scalar.activation(ln_r[:], ln_ve[:], ACT.Abs_reciprocal_sqrt).then_inc(ln_r0_ready, 1)
                    act.wait_ge(u_scaled, g + 1)
                    nc.scalar.activation(work[0][:], work[0][:], ACT.Gelu_apprx_tanh).then_inc(ug_ready, 1)
            stepped(act, KC // 2, u_pair)

            def a_step(j):
                split_hi(2 * j + (N_GATE_A + 1), 1)
                if not later(j):
                    copy_a(KC - 1)
                act.wait_ge(ga_scaled, j + 1)
                nc.scalar.activation(work[2][:], work[2][:], ACT.Sigmoid).then_inc(gate_a_ready, 1)
                split_hi(2 * j + (N_GATE_A + 2), 0)
            stepped(act, KC, a_step)
            for c in range(KC):
                act.wait_ge(m_ready, c + 1)
                nc.scalar.copy(h_hi[:, c, :], merged[:, c, :]).then_inc(m_hi_ready, 1)

            for c in range(KC):
                split_hi(c + (N_MERGE + 1), 1 - c % 2)
                act.wait_ge(x1_ready, c + 1)
                nc.scalar.activation(ffn_hi[:, c, :], resid[:, c, :], ACT.Copy,
                                     scale=vecs[:, V_FFN, c:c + 1]).then_inc(ffn_hi_ready, 1)
                if c:
                    act.wait_ge(ssq_step, c)
                nc.scalar.activation(work[1][:], resid[:, c, :], ACT.Square).then_inc(x1_sq, 1)

            for p, parts in enumerate(PARTS):
                def ff_step(j):
                    n = N_PART[p] + 2 * j
                    k = act_before[p] + j
                    split_hi(n + 1, 1)
                    if p == 0 and not later(j):
                        rms_guess(slice(0, T), 2)
                    act.wait_ge(ff_scaled, k + 1)
                    nc.scalar.activation(work[0][:], work[0][:], ACT.Silu).then_inc(silu_ready, 1)
                    split_hi(n + 2, 0)
                    act.wait_ge(act_raw, k + 1)
                    nc.scalar.copy(act_hi[:, j, :], work[1][:]).then_inc(act_hi_ready, 1)
                stepped(act, parts, ff_step)
                n_down = N_PART[p] + 2 * parts
                if p < len(PARTS) - 1:
                    with act.Fori(0, KC // 2) as k:
                        for i in range(2):
                            split_hi(2 * k + (n_down + 1 + i), 1 - i)
            split_hi(n_tail + 1, 1)
            def tail_hi(c):
                act.wait_ge(w_loaded[c % 2], 8 * (n_tail + c - c % 2) + 16)
                nc.scalar.copy(tail_weight(c)[0], w_raw[c % 2][:, 0:last_parts, :]).then_inc(w_hi_ready, 1)
            for c in range(2, 6):
                tail_hi(c)
            act.wait_ge(act_lo_ready, FC)
            for half in range(2):
                s = slice(half * H, half * H + H)
                for c in range(KC):
                    q = KC * half + c
                    act.wait_ge(down_ready, KC * (len(PARTS) - 1) + q + 1)
                    if c:
                        act.wait_ge(ssq_step, KC + (KC - 1) * half + c)
                    nc.scalar.activation(work[1][:, s], resid[:, c, s], ACT.Square).then_inc(x1_sq, 1)
                    if q < 2:
                        tail_hi(6 + q)
                    if q == KC + 1:
                        rms_guess(slice(0, H), 3)
            rms_guess(slice(H, T), 4)

        @block.vector
        def _(dve):
            def split_lo(n, i):
                dve.wait_ge(w_hi_ready, n + 1)
                if not isinstance(n, int) or n >= 2:
                    dve.wait_ge(proj_done, 2 * n - 2)
                nc.vector.tensor_tensor(w_lo[i][:], w_raw[i][:], f32(w_hi[i][:]), ALU.subtract
                                        ).then_inc(w_lo_ready, 1)

            def inverse_rms(s, count):
                dve.wait_ge(ssq_done, count)
                nc.vector.tensor_scalar(work[0][:, s], ps_a[:, s], 1.0 / D, EPS, ALU.mult, ALU.add
                                        ).then_inc(ve_ready, 1)
                dve.wait_ge(r0_ready, count)
                nc.vector.tensor_tensor(work[2][:, s], inv_rms[:, s], inv_rms[:, s], ALU.mult).then_inc(newton, 1)
                dve.wait_ge(newton, 2 * count - 1)
                nc.vector.scalar_tensor_tensor(out=work[2][:, s], in0=work[0][:, s], scalar=-0.5, in1=work[2][:, s],
                                               op0=ALU.mult, op1=ALU.mult).then_inc(newton, 1)
                dve.wait_ge(newton, 2 * count)
                nc.vector.scalar_tensor_tensor(out=inv_rms[:, s], in0=work[2][:, s], scalar=1.5, in1=inv_rms[:, s],
                                               op0=ALU.add, op1=ALU.mult).then_inc(rms_ready, 1)
                dve.wait_ge(rms_ready, count)

            def times_inv_rms(out, i, scaled):
                nc.vector.tensor_tensor(out, proj[i][:], inv_rms[:], ALU.mult).then_inc(scaled, 1)

            nc.vector.memset(keep[:], 1.0).then_inc(lb_step, 1)
            nc.vector.memset(scores[:], 0.0).then_inc(lb_step, 1)
            for c in range(KC):
                dve.wait_ge(h_hi_ready, c + 1)
                nc.vector.scalar_tensor_tensor(out=h_lo[:, c, :], in0=x_in[:, c, :], scalar=vecs[:, V_MIX, c:c + 1],
                                               in1=f32(h_hi[:, c, :]), op0=ALU.mult, op1=ALU.subtract
                                               ).then_inc(h_lo_ready, 1)
                if c == 0:
                    split_lo(0, 0)
            split_lo(1, 1)
            dve.wait_ge(vec_loaded, 16)
            dve.wait_ge(lb_step, 2)
            nc.vector.memset(chunks(keep[:])[:, :, 0:1], 0.0)
            nc.vector.tensor_tensor(lb_tmp[:, 0, :], vecs[:, V_LB0, :], vecs[:, V_LB1, :], ALU.max).then_inc(lb_exp, 1)
            dve.wait_ge(lb_exp, 1)
            nc.vector.tensor_tensor(lb_tmp[:, 1:3, :], vecs[:, V_LB0:V_LB1 + 1, :],
                                    lb_tmp[:, 0:1, :].broadcast_to([P, 2, KC]), ALU.subtract).then_inc(lb_step, 1)
            dve.wait_ge(lb_exp, 2)
            nc.vector.tensor_tensor(lb_tmp[:, 3, :], lb_tmp[:, 1, :], lb_tmp[:, 2, :], ALU.add).then_inc(lb_step, 1)
            dve.wait_ge(lb_step, 4)
            nc.vector.reciprocal(lb_tmp[:, 3, :], lb_tmp[:, 3, :]).then_inc(lb_step, 1)
            dve.wait_ge(lb_step, 5)
            nc.vector.tensor_tensor(lb[:], lb_tmp[:, 1, :], lb_tmp[:, 3, :], ALU.mult).then_inc(lb_step, 1)
            dve.wait_ge(lb_step, 6)
            nc.vector.tensor_scalar(one_minus_lb[:], lb[:], -1.0, 1.0, ALU.mult, ALU.add).then_inc(lb_step, 1)
            dve.wait_ge(lb_step, 7)
            dve.wait_ge(sq_ready, 1)
            for c in range(1, KC - POOL_SQUARES):
                dve.wait_ge(sq_ready, c + 1)
                if c > 1:
                    dve.wait_ge(ssq_first, c - 1)
                nc.vector.tensor_tensor(squares[:, POOL_SQUARES, :], squares[:, POOL_SQUARES, :],
                                        squares[:, POOL_SQUARES + c, :], ALU.add).then_inc(ssq_first, 1)
            inverse_rms(slice(0, T), 1)

            def head(h, own=True):
                n = 4 * h
                small = later(h)
                if small:
                    split_lo(n + 1, 1)
                if small:
                    dve.wait_ge(i_turned, h)
                    if not isinstance(h, int) or h >= 2:
                        dve.wait_ge(o_ready, h - 1)
                    nc.vector.tensor_copy(i_tok[:], ps_a[:]).then_inc(i_tok_ready, 1)
                dve.wait_ge(proj_done, 2 * n + 2)
                if own:
                    if small:
                        dve.wait_ge(exp_mid, 2 * h)
                    times_inv_rms(fgt[:], 0, f_scaled)
                else:
                    times_inv_rms(merged[:, 0, :], 0, gb_scaled)
                split_lo(n + 2, 0)
                if small:
                    dve.wait_ge(k_turned, h)
                    nc.vector.tensor_copy(k_tok[:, 0:T - P], ps_b[:, 0:T - P]).then_inc(k_tok_ready, 1)
                if own:
                    dve.wait_ge(sig_ready, h + 1)
                    nc.vector.tensor_scalar(fgt[:], fgt[:], one_minus_lb[:, bass.ds(h, 1)], lb[:, bass.ds(h, 1)], ALU.mult, ALU.add
                                            ).then_inc(f_ready, 1)
                    dve.wait_ge(f_ready, h + 1)
                    nc.vector.tensor_scalar(key[:], fgt[:], -1.0, 1.0, ALU.mult, ALU.add).then_inc(key_ready, 1)
                if own:
                    dve.wait_ge(logf_ready, h + 1)
                    if small:
                        dve.wait_ge(exp_out, 2 * h)
                    nc.vector.tensor_tensor_scan(cum[:], keep[:], fgt[:], 0.0, ALU.mult, ALU.add
                                                 ).then_inc(cum_ready, 1)
                    dve.wait_ge(cum_ready, h + 1)
                    nc.vector.tensor_tensor(chunks(fgt[:]), chunks(cum[:]),
                                            chunks(cum[:])[:, :, CH // 2 - 1:CH // 2].broadcast_to([P, NCH, CH]),
                                            ALU.subtract).then_inc(mid_ready, 1)
                    nc.vector.tensor_tensor(chunks(to_last[:]),
                                            chunks(cum[:])[:, :, CH - 1:CH].broadcast_to([P, NCH, CH]),
                                            chunks(cum[:]), ALU.subtract).then_inc(last_ready, 1)
                if small:
                    dve.wait_ge(ds_done, h)
                    if not isinstance(h, int) or h >= 2:
                        dve.wait_ge(o_done, h - 1)
                    ds = supers(ps_a[:])
                    nc.vector.tensor_copy(state[:, 0, :], ds[:, 0, :]).then_inc(state_step, 1)
                    for c in range(1, NSC - 1):
                        dve.wait_ge(state_step, (NSC - 1) * (h - 1) + c)
                        nc.vector.scalar_tensor_tensor(out=state[:, c, :], in0=state[:, c - 1, :],
                                                       scalar=dec2[:, c:c + 1], in1=ds[:, c, :],
                                                       op0=ALU.mult, op1=ALU.add).then_inc(state_step, 1)
                dve.wait_ge(proj_done, 2 * n + 4)
                if own:
                    if small:
                        dve.wait_ge(q_cum_ready, h)
                    nc.vector.scalar_tensor_tensor(out=qry[:], in0=proj[1][:], scalar=DK_SCALE, in1=inv_rms[:],
                                                   op0=ALU.mult, op1=ALU.mult).then_inc(qry_ready, 1)
                else:
                    times_inv_rms(merged[:, 1, :], 1, gb_scaled)
                if small:
                    dve.wait_ge(const_ready, 3)
                    dve.wait_ge(diag_done, h)
                    nc.vector.copy_predicated(scores[:], causal[:].bitcast(I32)[:, None, :].broadcast_to([P, NSC, P]),
                                              supers(ps_b[:])).then_inc(diag_ready, 1)
                split_lo(n + 3, 1)
                if own:
                    dve.wait_ge(exp_mid, 2 * h + 1)
                    nc.vector.tensor_tensor(k_mid[:], k_mid[:], key[:], ALU.mult).then_inc(k_mid_ready, 1)
                    dve.wait_ge(exp_mid, 2 * h + 2)
                    dve.wait_ge(qry_ready, h + 1)
                    nc.vector.tensor_tensor(q_mid[:], q_mid[:], qry[:], ALU.mult).then_inc(q_mid_ready, 1)
                if small:
                    dve.wait_ge(cross_done, h)
                    dve.wait_ge(diag_ready, h)
                    nc.vector.tensor_copy(scores[0:CH, :, CH:P],
                                          ps_a[0:CH, 0:H].rearrange("p (c t) -> p c t", t=CH)
                                          ).then_inc(cross_ready, 1)
                dve.wait_ge(proj_done, 2 * n + 6)
                if own:
                    if small:
                        dve.wait_ge(i_turned, h)
                    times_inv_rms(i_feat[:], 0, i_feat_ready)
                else:
                    times_inv_rms(merged[:, 2, :], 0, gb_scaled)
                split_lo(n + 4, 0)
                if own:
                    dve.wait_ge(exp_out, 2 * h + 1)
                    nc.vector.tensor_tensor(k_end[:], k_end[:], key[:], ALU.mult).then_inc(k_end_ready, 1)
                    dve.wait_ge(exp_out, 2 * h + 2)
                    nc.vector.tensor_tensor(q_cum[:], q_cum[:], qry[:], ALU.mult).then_inc(q_cum_ready, 1)
                    dve.wait_ge(dec_ready, h + 1)
                    d = dec[:].rearrange("p (c two) -> p c two", two=2)
                    ke = k_end[:].rearrange("p (c two t) -> p c two t", two=2, t=CH)
                    ko = k_out[:].rearrange("p (c two t) -> p c two t", two=2, t=CH)
                    qc = q_cum[:].rearrange("p (c two t) -> p c two t", two=2, t=CH)
                    qs = q_sc[:].rearrange("p (c two t) -> p c two t", two=2, t=CH)
                    if small:
                        dve.wait_ge(k_turned, h)
                    dve.wait_ge(k_end_ready, h + 1)
                    nc.vector.tensor_tensor(ko[:, :, 0, :], ke[:, :, 0, :],
                                            d[:, :, 1:2].broadcast_to([P, NSC, CH]), ALU.mult).then_inc(k_out_ready, 1)
                    nc.vector.tensor_copy(ko[:, :, 1, :], ke[:, :, 1, :]).then_inc(k_out_ready, 1)
                    if small:
                        dve.wait_ge(o_done, h)
                    dve.wait_ge(q_cum_ready, h + 1)
                    nc.vector.tensor_tensor(qs[:, :, 1, :], qc[:, :, 1, :],
                                            d[:, :, 0:1].broadcast_to([P, NSC, CH]), ALU.mult).then_inc(q_sc_ready, 1)
                    nc.vector.tensor_tensor(dec2[:], d[:, :, 0], d[:, :, 1], ALU.mult).then_inc(dec2_ready, 1)
                    nc.vector.tensor_copy(qs[:, :, 0, :], qc[:, :, 0, :]).then_inc(q_sc_ready, 1)
                if small:
                    dve.wait_ge(osq_ready, h)
                    dve.wait_ge(gate_ready, h)
                    nc.vector.scalar_tensor_tensor(out=o_raw[:, h - 1, :], in0=ps_b[:],
                                                   scalar=vecs[:, V_HG, bass.ds(h - 1, 1)], in1=s_gate[:],
                                                   op0=ALU.mult, op1=ALU.mult).then_inc(ob_ready, 1)
                    dve.wait_ge(osum_done, h)
                    nc.vector.tensor_scalar(o_sq[:], ps_a[:], 1.0 / P, EPS, ALU.mult, ALU.add).then_inc(ove_ready, 1)
                    dve.wait_ge(or0_ready, h)
                    nc.vector.tensor_tensor(i_tok[:], k_tok[:], k_tok[:], ALU.mult).then_inc(onewton, 1)
                    dve.wait_ge(onewton, 3 * h - 2)
                    nc.vector.scalar_tensor_tensor(out=i_tok[:], in0=o_sq[:], scalar=-0.5, in1=i_tok[:],
                                                   op0=ALU.mult, op1=ALU.mult).then_inc(onewton, 1)
                    dve.wait_ge(onewton, 3 * h - 1)
                    nc.vector.scalar_tensor_tensor(out=k_tok[:], in0=i_tok[:], scalar=1.5, in1=k_tok[:],
                                                   op0=ALU.add, op1=ALU.mult).then_inc(onewton, 1)
                    dve.wait_ge(onewton, 3 * h)
                    nc.vector.tensor_tensor(o_raw[:, h - 1, :], o_raw[:, h - 1, :], k_tok[:], ALU.mult
                                            ).then_inc(o_ready, 1)
                dve.wait_ge(proj_done, 2 * n + 8)
                if own:
                    times_inv_rms(s_gate[:], 1, g_scaled)
                else:
                    times_inv_rms(merged[:, 3, :], 1, gb_scaled)

            head(0)
            head(1)
            with dve.Fori(2, HEADS) as h:
                head(h)
            head(HEADS, own=False)

            with dve.Fori(0, 2) as k:
                for i in range(2):
                    split_lo(2 * k + (N_GATE_B + 5 + i), 1 - i)
                    for j in range(2):
                        c = 4 * k + (2 * i + j)
                        dve.wait_ge(o_hi_ready, c + 1)
                        nc.vector.tensor_tensor(o_lo[:, c, :], o_raw[:, c, :], f32(o_hi[:, c, :]), ALU.subtract
                                                ).then_inc(o_lo_ready, 1)
                    dve.wait_ge(proj_done, 4 * k + (2 * (N_GATE_B + 4 + i) + 2))
                    times_inv_rms(merged[:, 2 * k + (4 + i), :], i, gb_scaled)
            with dve.Fori(0, KC // 2) as k:
                for i in range(2):
                    split_lo(2 * k + (N_OUT_B + 1 + i), 1 - i)
                    dve.wait_ge(proj_done, 4 * k + (2 * (N_OUT_B + i) + 2))
                    dve.wait_ge(gate_b_ready, 2 * k + (i + 1))
                    nc.vector.tensor_tensor(merged[:, 2 * k + i, :], proj[i][:], merged[:, 2 * k + i, :], ALU.mult
                                            ).then_inc(part_ready, 1)

            v_rows = v_tok[:]

            def take_v(j, ps):
                dve.wait_ge(v_turned, j + 1)
                nc.vector.tensor_copy(v_rows[:, j, :, :], supers(ps[:])).then_inc(v_tok_ready, 1)

            def group_stats(part):
                dve.wait_ge(v_tok_ready, 4 * part + 4)
                for t in range(NSC):
                    nc.vector.bn_stats(stats[:, t, part, :], v_rows[:, 4 * part:4 * part + 4, t, :]
                                       ).then_inc(bn_step, 1)

            def v_pair(k):
                for i in range(2):
                    split_lo(2 * k + (N_V + 1 + i), 1 - i)
                    if i or later(k):
                        take_v(2 * k + (i - 1), [ps_b, ps_a][i])
                    else:
                        dve.wait_ge(rowsum_done, 1)
                        dve.wait_ge(bsp_loaded, 16)
                        for g in range(KC):
                            nc.vector.scalar_tensor_tensor(out=mix_bias[:, g, :], in0=supers(ps_b[:])[:, g, :],
                                                           scalar=vecs[:, V_LNB, g:g + 1], in1=b_bcast[:, g, :],
                                                           op0=ALU.mult, op1=ALU.add).then_inc(bias_ready, 1)
                    if isinstance(k, int) and k == KC // 2 - 1 and i == 0:
                        group_stats(0)
                    if later(k):
                        dve.wait_ge(v_turned, 2 * k + (i - 1))
                    dve.wait_ge(proj_done, 4 * k + (2 * (N_V + i) + 2))
                    times_inv_rms(work[i][:], i, v_scaled)
            stepped(dve, KC // 2 - 1, v_pair)
            v_pair(KC // 2 - 1)

            def mix(g, ps):
                dve.wait_ge(mixed_done, g + 1)
                if later(g):
                    dve.wait_ge(a_hi_ready, g)
                nc.vector.scalar_tensor_tensor(
                    out=supers(work[1][:]), in0=supers(ps[:]), scalar=vecs[:, V_LNG, bass.ds(g, 1)],
                    in1=mix_bias[:, g, :][:, None, :].broadcast_to([P, NSC, P]) if isinstance(g, int)
                    else mix_bias[:, bass.ds(g, 1), :].broadcast_to([P, NSC, P]),
                    op0=ALU.mult, op1=ALU.add).then_inc(mix_ready, 1)
                dve.wait_ge(mix_ready, g + 1)
                dve.wait_ge(ug_ready, g + 1)
                nc.vector.tensor_tensor(work[1][:], work[1][:], work[0][:], ALU.mult).then_inc(a_raw_ready, 1)
                dve.wait_ge(a_hi_ready, g + 1)
                nc.vector.tensor_tensor(a_lo[:, g, :], work[1][:], f32(a_hi[:, g, :]), ALU.subtract
                                        ).then_inc(a_lo_ready, 1)

            def layer_norm_stats():
                take_v(KC - 1, ps_b)
                group_stats(1)
                dve.wait_ge(bn_step, 2 * NSC)
                for t in range(NSC):
                    nc.vector.bn_aggr(mean_var[:, t, :], stats[:, t, :, :].rearrange("p a b -> p (a b)")
                                      ).then_inc(bn_step, 1)
                dve.wait_ge(bn_step, 3 * NSC)
                nc.vector.tensor_scalar(ln_ve[:], mean_var[:, :, 1], EPS, None, ALU.add).then_inc(stat_step, 1)
                dve.wait_ge(ln_r0_ready, 1)
                nc.vector.tensor_tensor(ln_t[:], ln_r[:], ln_r[:], ALU.mult).then_inc(stat_step, 1)
                dve.wait_ge(stat_step, 2)
                nc.vector.scalar_tensor_tensor(out=ln_t[:], in0=ln_ve[:], scalar=-0.5, in1=ln_t[:],
                                               op0=ALU.mult, op1=ALU.mult).then_inc(stat_step, 1)
                dve.wait_ge(stat_step, 3)
                nc.vector.scalar_tensor_tensor(out=ln_r[:], in0=ln_t[:], scalar=1.5, in1=ln_r[:],
                                               op0=ALU.add, op1=ALU.mult).then_inc(stat_step, 1)
                dve.wait_ge(stat_step, 4)

            def u_pair(k):
                for i in range(2):
                    g = 2 * k + i
                    split_lo(g + (N_U + 1), 1 - i)
                    if i or later(k):
                        mix(g - 1, [ps_b, ps_a][i])
                    else:
                        layer_norm_stats()
                    nc.vector.tensor_tensor(supers(work[2][:]), v_rows[:, g, :, :],
                                            mean_var[:, :, 0:1].broadcast_to([P, NSC, P]), ALU.subtract
                                            ).then_inc(z_centred, 1)
                    dve.wait_ge(z_centred, g + 1)
                    nc.vector.tensor_tensor(supers(work[2][:]), supers(work[2][:]),
                                            ln_r[:, :, None].broadcast_to([P, NSC, P]), ALU.mult
                                            ).then_inc(z_ready, 1)
                    dve.wait_ge(proj_done, 2 * g + (2 * N_U + 2))
                    if not (i or later(k)):
                        dve.wait_ge(v_turned, KC)
                    times_inv_rms(work[0][:], i, u_scaled)
            stepped(dve, KC // 2, u_pair)

            def a_step(j):
                split_lo(2 * j + (N_GATE_A + 1), 1)
                if not later(j):
                    mix(KC - 1, ps_b)
                dve.wait_ge(proj_done, 4 * j + (2 * N_GATE_A + 2))
                times_inv_rms(work[2][:], 0, ga_scaled)
                split_lo(2 * j + (N_GATE_A + 2), 0)
                if isinstance(j, int) and j == KC - 1:
                    for c in range(KC - 1):
                        merged_low(c)
                dve.wait_ge(proj_done, 4 * j + (2 * N_GATE_A + 4))
                dve.wait_ge(gate_a_ready, j + 1)
                nc.vector.tensor_tensor(work[0][:], proj[1][:], work[2][:], ALU.mult).then_inc(ya_ready, 1)
                dve.wait_ge(ya_ready, j + 1)
                nc.vector.tensor_tensor(merged[:, j, :], merged[:, j, :], work[0][:], ALU.add).then_inc(m_ready, 1)

            def merged_low(c):
                dve.wait_ge(m_hi_ready, c + 1)
                nc.vector.tensor_tensor(merged_lo[:, c, :], merged[:, c, :], f32(h_hi[:, c, :]), ALU.subtract
                                        ).then_inc(m_lo_ready, 1)
            stepped(dve, KC - 1, a_step)
            a_step(KC - 1)
            merged_low(KC - 1)

            for c in range(KC):
                split_lo(N_MERGE + 1 + c, 1 - c % 2)
                dve.wait_ge(proj_done, 2 * (N_MERGE + c) + 2)
                dve.wait_ge(x_again[c], 16)
                nc.vector.tensor_tensor(resid[:, c, :], proj[c % 2][:], resid[:, c, :], ALU.add).then_inc(x1_ready, 1)
                dve.wait_ge(ffn_hi_ready, c + 1)
                nc.vector.scalar_tensor_tensor(out=h_lo[:, c, :], in0=resid[:, c, :], scalar=vecs[:, V_FFN, c:c + 1],
                                               in1=f32(ffn_hi[:, c, :]), op0=ALU.mult, op1=ALU.subtract
                                               ).then_inc(ffn_lo_ready, 1)
                dve.wait_ge(x1_sq, c + 1)
                if c:
                    dve.wait_ge(ssq_step, c)
                    nc.vector.tensor_tensor(work[0][:], work[0][:], work[1][:], ALU.add).then_inc(ssq_step, 1)
                else:
                    nc.vector.tensor_copy(work[0][:], work[1][:]).then_inc(ssq_step, 1)

            for p, parts in enumerate(PARTS):
                def ff_step(j):
                    n = N_PART[p] + 2 * j
                    k = act_before[p] + j
                    split_lo(n + 1, 1)
                    if p == 0 and not later(j):
                        inverse_rms(slice(0, T), 2)
                    dve.wait_ge(proj_done, 2 * n + 2)
                    times_inv_rms(work[0][:], 0, ff_scaled)
                    split_lo(n + 2, 0)
                    dve.wait_ge(silu_ready, k + 1)
                    nc.vector.tensor_tensor(work[0][:], work[0][:], inv_rms[:], ALU.mult).then_inc(silu_scaled, 1)
                    dve.wait_ge(silu_scaled, k + 1)
                    dve.wait_ge(proj_done, 2 * n + 4)
                    nc.vector.tensor_tensor(work[1][:], proj[1][:], work[0][:], ALU.mult).then_inc(act_raw, 1)
                    dve.wait_ge(act_hi_ready, k + 1)
                    nc.vector.tensor_tensor(act_lo[:, j, :], work[1][:], f32(act_hi[:, j, :]), ALU.subtract
                                            ).then_inc(act_lo_ready, 1)
                stepped(dve, parts, ff_step)
                n_down = N_PART[p] + 2 * parts
                if p < len(PARTS) - 1:
                    with dve.Fori(0, KC // 2) as k:
                        for i in range(2):
                            split_lo(2 * k + (n_down + 1 + i), 1 - i)
                            dve.wait_ge(proj_done, 4 * k + (2 * (n_down + i) + 2))
                            nc.vector.tensor_tensor(resid[:, 2 * k + i, :], proj[i][:], resid[:, 2 * k + i, :], ALU.add
                                                    ).then_inc(down_ready, 1)
            def tail_lo(c):
                dve.wait_ge(w_hi_ready, n_tail + c + 1)
                hi, lo = tail_weight(c)
                nc.vector.tensor_tensor(lo, w_raw[c % 2][:, 0:last_parts, :], f32(hi), ALU.subtract
                                        ).then_inc(w_lo_ready, 1)

            def store_ready(s, c):
                nc.vector.scalar_tensor_tensor(out=resid[:, c, s], in0=resid[:, c, s],
                                               scalar=vecs[:, V_FIN, c:c + 1], in1=inv_rms[:, s],
                                               op0=ALU.mult, op1=ALU.mult).then_inc(out_ready, 1)
            split_lo(n_tail + 1, 1)
            for c in range(2, 4):
                tail_lo(c)
            for half in range(2):
                s = slice(half * H, half * H + H)
                for c in range(KC):
                    q = KC * half + c
                    dve.wait_ge(tail_done, q + 1)
                    nc.vector.tensor_tensor(resid[:, c, s], tail_bank(q), resid[:, c, s], ALU.add
                                            ).then_inc(down_ready, 1)
                    if half == 0 and c + 4 < KC:
                        tail_lo(c + 4)
                    step = KC + (KC - 1) * half + c
                    if c < KC - 1:
                        dve.wait_ge(x1_sq, KC + q + 1)
                        if c:
                            dve.wait_ge(ssq_step, step)
                            nc.vector.tensor_tensor(work[0][:, s], work[0][:, s], work[1][:, s], ALU.add
                                                    ).then_inc(ssq_step, 1)
                        else:
                            nc.vector.tensor_copy(work[0][:, s], work[1][:, s]).then_inc(ssq_step, 1)
                    if q == KC + 1:
                        inverse_rms(slice(0, H), 3)
                    if half == 1 and 2 <= c < 6:
                        for cc in (2 * c - 4, 2 * c - 3):
                            store_ready(slice(0, H), cc)
            inverse_rms(slice(H, T), 4)
            for c in range(KC):
                store_ready(slice(H, T), c)

        @block.tensor
        def _(pe):
            def half_block(n, i, half, hi, lo, free=None, chunks_in=KC, wait_chunk=None, between=None):
                if half == 0:
                    pe.wait_ge(w_hi_ready, n + 1)
                    pe.wait_ge(w_lo_ready, n + 1)
                    if free is not None:
                        pe.wait_ge(*free)
                s = slice(half * H, half * H + H)
                for k in range(chunks_in):
                    if between is not None and k == between[0]:
                        between[1]()
                    if wait_chunk is not None:
                        wait_chunk(k, half)
                    nc.tensor.matmul(proj[i][:, s], w_hi[i][:, k, :], hi[:, k, s], start=(k == 0), stop=False)
                    nc.tensor.matmul(proj[i][:, s], w_hi[i][:, k, :], lo[:, k, s], start=False, stop=False)
                    last = nc.tensor.matmul(proj[i][:, s], w_lo[i][:, k, :], hi[:, k, s],
                                            start=False, stop=(k == chunks_in - 1))
                last.then_inc(proj_done, 1)

            def full_block(n, i, hi, lo, **kw):
                half_block(n, i, 0, hi, lo, **kw)
                half_block(n, i, 1, hi, lo, **kw)

            def first_block():
                pe.wait_ge(w_hi_ready, 1)
                pe.wait_ge(w_lo_ready, 1)
                for k in range(KC):
                    pe.wait_ge(h_hi_ready, k + 1)
                    pe.wait_ge(h_lo_ready, k + 1)
                    for half in range(2):
                        s = slice(half * H, half * H + H)
                        nc.tensor.matmul(proj[0][:, s], w_hi[0][:, k, :], h_hi[:, k, s], start=(k == 0), stop=False)
                        nc.tensor.matmul(proj[0][:, s], w_hi[0][:, k, :], h_lo[:, k, s], start=False, stop=False)
                        last = nc.tensor.matmul(proj[0][:, s], w_lo[0][:, k, :], h_hi[:, k, s],
                                                start=False, stop=(k == KC - 1))
                        if k == KC - 1:
                            last.then_inc(proj_done, 1)

            def tail_squares(half):
                s = slice(half * H, half * H + H)
                pe.wait_ge(ssq_step, KC + (KC - 1) * (half + 1))
                nc.tensor.matmul(ps_a[:, s], ones[:], work[0][:, s], start=True, stop=False)
                pe.wait_ge(x1_sq, KC + KC * (half + 1))
                nc.tensor.matmul(ps_a[:, s], ones[:], work[1][:, s], start=False, stop=True).then_inc(ssq_done, 1)

            def sum_squares(parts_of, wait):
                for half in range(2):
                    s = slice(half * H, half * H + H)
                    for t, part in enumerate(parts_of):
                        if half == 0:
                            pe.wait_ge(*wait[t])
                        last = nc.tensor.matmul(ps_a[:, s], ones[:], part[:, s], start=(t == 0),
                                                stop=(t == len(parts_of) - 1))
                last.then_inc(ssq_done, 1)

            def head(h, own=True):
                n = 4 * h
                small = later(h)
                first = isinstance(h, int) and h == 0

                def slot(b, half):
                    if own:
                        free = [(i_feat_ready, h), (g_scaled, h), (f_scaled, h + 1), (qry_ready, h + 1)][b]
                    else:
                        free = [(i_feat_ready, HEADS), (g_scaled, HEADS), (gb_scaled, 1), (gb_scaled, 2)][b]
                    if first and b < 2:
                        free = None
                    if first and b == 0:
                        if half == 0:
                            first_block()
                    else:
                        half_block(n + b, b % 2, half, h_hi, h_lo, free=free)

                slot(0, 0)
                if small:
                    pe.wait_ge(i_feat_ready, h)
                    if not isinstance(h, int) or h >= 2:
                        pe.wait_ge(ove_ready, h - 1)
                    for c in range(NSC):
                        last = nc.tensor.transpose(supers(ps_a[:])[:, c, :], supers(i_feat[:])[:, c, :], ident[:])
                    last.then_inc(i_turned, 1)
                slot(0, 1)
                if small:
                    pe.wait_ge(k_out_ready, 2 * h)
                    if not isinstance(h, int) or h >= 2:
                        pe.wait_ge(ob_ready, h - 1)
                    for c in range(NSC - 1):
                        last = nc.tensor.transpose(supers(ps_b[:])[:, c, :], supers(k_out[:])[:, c, :], ident[:])
                    last.then_inc(k_turned, 1)
                slot(1, 0)
                if small:
                    pe.wait_ge(i_tok_ready, h)
                    pe.wait_ge(k_tok_ready, h)
                    for c in range(NSC - 1):
                        last = nc.tensor.matmul(supers(ps_a[:])[:, c, :], supers(k_tok[:])[:, c, :],
                                                supers(i_tok[:])[:, c, :], start=True, stop=True)
                    last.then_inc(ds_done, 1)
                if first:
                    pe.wait_ge(const_ready, 1)
                    sum_squares([squares[:, 0, :], squares[:, POOL_SQUARES, :]],
                                [(sq_pool, 2 * POOL_SQUARES - 1), (ssq_first, KC - POOL_SQUARES - 1)])
                slot(1, 1)
                if small:
                    pe.wait_ge(k_mid_ready, h)
                    pe.wait_ge(q_mid_ready, h)
                    for c in range(NSC):
                        last = nc.tensor.matmul(supers(ps_b[:])[:, c, :], supers(k_mid[:])[:, c, :],
                                                supers(q_mid[:])[:, c, :], start=True, stop=True)
                    last.then_inc(diag_done, 1)
                slot(2, 0)
                if small:
                    pe.wait_ge(state_step, (NSC - 1) * h)
                    pe.wait_ge(k_end_ready, h)
                    pe.wait_ge(q_cum_ready, h)
                    for c in range(NSC):
                        last = nc.tensor.matmul(ps_a[0:CH, CH * c:CH * c + CH], chunks(k_end[:])[:, 2 * c, :],
                                                chunks(q_cum[:])[:, 2 * c + 1, :], start=True, stop=True)
                    last.then_inc(cross_done, 1)
                slot(2, 1)
                if small:
                    pe.wait_ge(diag_ready, h)
                    pe.wait_ge(cross_ready, h)
                    pe.wait_ge(q_sc_ready, 2 * h)
                    for c in range(NSC):
                        last = nc.tensor.matmul(supers(ps_b[:])[:, c, :], supers(i_tok[:])[:, c, :],
                                                scores[:, c, :], start=True, stop=(c == 0))
                        if c > 0:
                            last = nc.tensor.matmul(supers(ps_b[:])[:, c, :], state[:, c - 1, :],
                                                    supers(q_sc[:])[:, c, :], start=False, stop=True)
                    last.then_inc(o_done, 1)
                slot(3, 0)
                if small:
                    pe.wait_ge(osq_ready, h)
                    for half in range(2):
                        last = nc.tensor.matmul(ps_a[:, half * H:half * H + H], ones[:],
                                                o_sq[:, half * H:half * H + H], start=True, stop=True)
                    last.then_inc(osum_done, 1)
                slot(3, 1)

            head(0)
            head(1)
            with pe.Fori(2, HEADS) as h:
                head(h)
            head(HEADS, own=False)

            with pe.Fori(0, 2) as k:
                for i in range(2):
                    full_block(2 * k + (N_GATE_B + 4 + i), i, h_hi, h_lo, free=(gb_scaled, 2 * k + (3 + i)))

            def yb_pair(k):
                for i in range(2):
                    def wait_o(c, half):
                        if half == 0:
                            pe.wait_ge(o_hi_ready, c + 1)
                            pe.wait_ge(o_lo_ready, c + 1)
                    full_block(2 * k + (N_OUT_B + i), i, o_hi, o_lo,
                               free=(part_ready, 2 * k + (i - 1)) if later(k) else (gb_scaled, KC - 1 + i),
                               wait_chunk=None if later(k) or i else wait_o)
            stepped(pe, KC // 2, yb_pair)

            def turn_v(j, i):
                pe.wait_ge(vg_ready, j + 1)
                if later(j):
                    pe.wait_ge(v_tok_ready, j)
                ps = [ps_a, ps_b][i]
                for c in range(NSC):
                    last = nc.tensor.transpose(supers(ps[:])[:, c, :], supers(work[i][:])[:, c, :], ident[:])
                last.then_inc(v_turned, 1)

            def v_pair(k):
                for i in range(2):
                    n = 2 * k + (N_V + i)
                    free = (v_scaled, 2 * k + (i - 1)) if later(k) else (part_ready, KC - 1 + i)
                    half_block(n, i, 0, h_hi, h_lo, free=free)
                    if not (i or later(k)):
                        pe.wait_ge(const_ready, 4)
                        for half in range(2):
                            last = nc.tensor.matmul(ps_b[:, half * H:half * H + H], ones[:],
                                                    spatial_t[:, 4 * half:4 * half + 4, :].rearrange("p g t -> p (g t)"),
                                                    start=True, stop=True)
                        last.then_inc(rowsum_done, 1)
                    if i or later(k):
                        turn_v(2 * k + (i - 1), 1 - i)
                    half_block(n, i, 1, h_hi, h_lo)
            stepped(pe, KC // 2, v_pair)

            def mixing(g, i):
                pe.wait_ge(z_ready, g + 1)
                if later(g):
                    pe.wait_ge(mix_ready, g)
                else:
                    pe.wait_ge(v_tok_ready, KC - 1)
                ps = [ps_a, ps_b][i]
                for c in range(NSC):
                    rhs = spatial_t[:, g, :]
                    last = nc.tensor.matmul(supers(ps[:])[:, c, :], supers(work[2][:])[:, c, :], rhs,
                                            start=True, stop=True)
                last.then_inc(mixed_done, 1)

            def u_pair(k):
                for i in range(2):
                    n = 2 * k + (N_U + i)
                    free = (u_scaled, 2 * k + (i - 1)) if later(k) else (v_scaled, KC - 1 + i)
                    half_block(n, i, 0, h_hi, h_lo, free=free,
                               between=None if i or later(k) else (4, lambda: turn_v(KC - 1, 1)))
                    if i or later(k):
                        mixing(2 * k + (i - 1), 1 - i)
                    half_block(n, i, 1, h_hi, h_lo)
            stepped(pe, KC // 2, u_pair)

            def a_step(j):
                n = 2 * j + N_GATE_A
                half_block(n, 0, 0, h_hi, h_lo, free=(ga_scaled, j) if later(j) else (u_scaled, KC - 1))
                if not later(j):
                    mixing(KC - 1, 1)
                half_block(n, 0, 1, h_hi, h_lo)

                def wait_a(c, half):
                    if half == 0:
                        pe.wait_ge(a_hi_ready, c + 1)
                        pe.wait_ge(a_lo_ready, c + 1)
                full_block(n + 1, 1, a_hi, a_lo, free=(ya_ready, j) if later(j) else (u_scaled, KC),
                           wait_chunk=None if later(j) else wait_a)
            stepped(pe, KC, a_step)

            def out_pair(k):
                for i in range(2):
                    def wait_m(c, half):
                        if half == 0:
                            pe.wait_ge(m_hi_ready, c + 1)
                            pe.wait_ge(m_lo_ready, c + 1)
                    if later(k):
                        free = (x1_ready, 2 * k + (i - 1))
                    else:
                        free = [(ga_scaled, KC), (ya_ready, KC)][i]
                    full_block(2 * k + (N_MERGE + i), i, h_hi, merged_lo, free=free,
                               wait_chunk=None if later(k) or i else wait_m)
            stepped(pe, KC // 2, out_pair)

            def wait_ffn(c, half):
                if half == 0:
                    pe.wait_ge(ffn_hi_ready, c + 1)
                    pe.wait_ge(ffn_lo_ready, c + 1)

            for p, parts in enumerate(PARTS):
                def ff_step(j):
                    n = N_PART[p] + 2 * j
                    k = act_before[p] + j
                    if later(j):
                        free_gate, free_up = (ff_scaled, k), (act_raw, k)
                    elif p == 0:
                        free_gate, free_up = (x1_ready, KC - 1), (x1_ready, KC)
                    else:
                        free_gate, free_up = (down_ready, KC * p - 1), (down_ready, KC * p)
                    if p == 0 and not later(j):
                        half_block(n, 0, 0, ffn_hi, h_lo, free=free_gate, wait_chunk=wait_ffn)
                        sum_squares([work[0]], [(ssq_step, KC)])
                        half_block(n, 0, 1, ffn_hi, h_lo)
                    else:
                        full_block(n, 0, ffn_hi, h_lo, free=free_gate)
                    full_block(n + 1, 1, ffn_hi, h_lo, free=free_up)
                stepped(pe, parts, ff_step)
                n_down = N_PART[p] + 2 * parts
                done = act_before[p] + parts
                if p == len(PARTS) - 1:
                    continue

                def wait_act(c, half):
                    if half == 0:
                        pe.wait_ge(act_hi_ready, act_before[p] + c + 1)
                        pe.wait_ge(act_lo_ready, act_before[p] + c + 1)

                def down_pair(k):
                    for i in range(2):
                        if later(k):
                            free = (down_ready, 2 * k + (KC * p + i - 1))
                        else:
                            free = [(ff_scaled, done), (act_raw, done)][i]
                        full_block(2 * k + (n_down + i), i, act_hi, act_lo, free=free, chunks_in=parts,
                                   wait_chunk=None if later(k) or i else wait_act)
                stepped(pe, KC // 2, down_pair)

            for half in range(2):
                s = slice(half * H, half * H + H)
                for c in range(KC):
                    q = KC * half + c
                    if half == 0:
                        pe.wait_ge(w_hi_ready, n_tail + c + 1)
                        pe.wait_ge(w_lo_ready, n_tail + c + 1)
                    if q >= 4:
                        pe.wait_ge(down_ready, KC * (len(PARTS) - 1) + q - 3)
                    elif q == 0:
                        pe.wait_ge(ff_scaled, FC)
                    elif q == 2:
                        pe.wait_ge(act_raw, FC)
                    hi, lo = tail_weight(c)
                    for k in range(last_parts):
                        if q == 0:
                            pe.wait_ge(act_hi_ready, FC - last_parts + k + 1)
                            pe.wait_ge(act_lo_ready, FC - last_parts + k + 1)
                        nc.tensor.matmul(tail_bank(q), hi[:, k, :], act_hi[:, k, s], start=(k == 0), stop=False)
                        nc.tensor.matmul(tail_bank(q), hi[:, k, :], act_lo[:, k, s], start=False, stop=False)
                        last = nc.tensor.matmul(tail_bank(q), lo[:, k, :], act_hi[:, k, s], start=False,
                                                stop=(k == last_parts - 1))
                    last.then_inc(tail_done, 1)
                    if q == KC + 1:
                        tail_squares(0)
            tail_squares(1)

def kernel(x, norm_mix_g, w_in, gmlp_ln_g, gmlp_ln_b, gmlp_w_s, gmlp_b_s, hgrn_lb_table, hgrn_norm_g,
           w_branch_a, w_branch_b, w_out, norm_ffn_g, w_gate_up, w_down, norm_final_g):
    import numpy as np
    import concourse.bacc as bacc
    from concourse.bass_utils import run_bass_kernel_spmd

    def blocks(w):
        w = np.asarray(w)
        return w.reshape(w.shape[0] // P, P, w.shape[1] // P, P).transpose(2, 1, 0, 3)

    x = np.asarray(x)
    w_in_b = blocks(np.asarray(w_in)[0])
    u, v, q, f, i, g, ga, gb = (w_in_b[KC * k:KC * k + KC] for k in range(8))
    wa, wb, wo = (blocks(np.asarray(w)[0]) for w in (w_branch_a, w_branch_b, w_out))
    gu, dn = blocks(np.asarray(w_gate_up)[0]), blocks(np.asarray(w_down)[0])
    stream = np.zeros((N_BLOCKS, P, KC, P), np.float32)
    for h in range(HEADS):
        for b, w in enumerate((f, q, i, g)):
            stream[N_HEAD + 4 * h + b] = w[h]
    for c in range(KC):
        stream[N_GATE_B + c] = gb[c]
        stream[N_OUT_B + c] = wb[c]
        stream[N_V + c] = v[c]
        stream[N_U + c] = u[c]
        stream[N_GATE_A + 2 * c] = ga[c]
        stream[N_GATE_A + 2 * c + 1] = wa[c]
        stream[N_MERGE + c] = wo[c]
    at = 0
    for p, parts in enumerate(PARTS):
        for j in range(parts):
            stream[N_PART[p] + 2 * j] = gu[at + j]
            stream[N_PART[p] + 2 * j + 1] = gu[FC + at + j]
        for c in range(KC):
            stream[N_PART[p] + 2 * parts + c, :, :parts] = dn[c][:, at:at + parts]
        at += parts
    per_feature = [np.asarray(norm_mix_g)[0], np.asarray(hgrn_lb_table)[0], np.asarray(hgrn_lb_table)[1],
                   np.asarray(hgrn_norm_g)[0], np.asarray(gmlp_ln_g)[0], np.asarray(gmlp_ln_b)[0],
                   np.asarray(norm_ffn_g)[0], np.asarray(norm_final_g)]
    arrays = {
        "x_t": np.ascontiguousarray(x[0].T.reshape(KC, P, T).transpose(1, 0, 2)),
        "w_stream": stream,
        "vectors": np.ascontiguousarray(np.stack([a.reshape(KC, P).T for a in per_feature], axis=1)),
        "w_spatial": np.ascontiguousarray(np.asarray(gmlp_w_s)[0].transpose(2, 0, 1)),
        "b_spatial": np.ascontiguousarray(np.asarray(gmlp_b_s)[0].reshape(1, KC * P)),
    }
    nc = bacc.Bacc("TRN2", target_bir_lowering=False, num_devices=1)
    args = [nc.dram_tensor(name, a.shape, F32, kind="ExternalInput").ap() for name, a in arrays.items()]
    out_t = nc.dram_tensor("out_t", (P, KC, T), F32, kind="ExternalOutput").ap()
    build(nc, *args, out_t)
    r = run_bass_kernel_spmd(nc, [arrays], core_ids=[0])
    out = np.asarray(r.results[0]["out_t"])
    return np.ascontiguousarray(out.transpose(1, 0, 2).reshape(D, T).T.reshape(1, T, D))
```

```python
from contextlib import ExitStack

import concourse.bass as bass
from concourse import mybir

F32 = mybir.dt.float32
F32R = mybir.dt.float32r
I32 = mybir.dt.int32
ACT = mybir.ActivationFunctionType
ALU = mybir.AluOpType

P = 128
T = 1024
H = T // 2
D = 1024
KC = D // P
HEADS = 8
CH = 64
NCH = T // CH
NSC = T // P
D_FF = -(-(8 * D) // (3 * 256)) * 256
FC = D_FF // P
EPS = 1e-6
DK_SCALE = float(P) ** -0.5

PARTS = [8, 7, 7]
assert sum(PARTS) == FC

N_HEAD = 0
N_GATE_B = N_HEAD + 4 * HEADS
N_OUT_B = N_GATE_B + KC
N_V = N_OUT_B + KC
N_U = N_V + KC
N_GATE_A = N_U + KC
N_MERGE = N_GATE_A + 2 * KC
N_PART = []
_n = N_MERGE + KC
for _p in PARTS:
    N_PART.append(_n)
    _n += 2 * _p + KC
N_BLOCKS = _n

POOL_SQUARES = 3

V_MIX, V_LB0, V_LB1, V_HG, V_LNG, V_LNB, V_FFN, V_FIN = range(8)


def build(nc, x_t, w_stream, vectors, w_spatial, b_spatial, out_t):
    with ExitStack() as ctx:
        def sb(name, shape, dt=F32, stack=ctx):
            return stack.enter_context(nc.sbuf_tensor(name, shape, dt))

        def sem(name):
            return ctx.enter_context(nc.semaphore(name))

        vecs = sb("vecs", [P, 8, KC])
        lb = sb("lb", [P, KC])
        one_minus_lb = sb("one_minus_lb", [P, KC])
        lb_tmp = sb("lb_tmp", [P, 4, KC])
        ones = sb("ones", [P, P])
        ones_r = sb("ones_r", [P, P], F32R)
        ident = sb("ident", [P, P])
        causal = sb("causal", [P, P])
        dec = sb("dec", [P, NCH])
        dec2 = sb("dec2", [P, NSC])
        inv_rms = sb("inv_rms", [P, T])
        rms_tok = sb("rms_tok", [P, NSC])
        stats = sb("stats", [P, NSC, 2, 6])
        mean_var = sb("mean_var", [P, NSC, 2])
        ln_ve = sb("ln_ve", [P, NSC])
        ln_r = sb("ln_r", [P, NSC])
        ln_t = sb("ln_t", [P, NSC])
        spatial_t = sb("spatial_t", [P, KC, P])
        w_raw = [sb(f"w_raw{i}", [P, KC, P]) for i in range(2)]
        w_hi = [sb(f"w_hi{i}", [P, KC, P], F32R) for i in range(2)]
        w_lo = [sb(f"w_lo{i}", [P, KC, P], F32R) for i in range(2)]
        h_hi = sb("h_hi", [P, KC, T], F32R)
        h_lo = sb("h_lo", [P, KC, T], F32R)

        def alias(name, shape, dt=F32):
            with nc.sbuf_tensor(name, shape, dt) as t:
                return t
        x_in = alias("x_in", [P, KC, T])
        o_raw = alias("o_raw", [P, KC, T])
        o_lo = alias("o_lo", [P, KC, T], F32R)
        v_tok = alias("v_tok", [P, KC, NSC, P])
        a_hi = alias("a_hi", [P, KC, T], F32R)
        resid = sb("resid", [P, KC, T])
        work = [sb(f"work{i}", [P, T]) for i in range(3)]
        q_sc, s_gate, o_sq = work
        with ExitStack() as heads:
            def hb(name, shape=(P, T)):
                return sb(name, list(shape), F32, heads)
            fgt, key, cum, to_last = hb("fgt"), hb("key"), hb("cum"), hb("to_last")
            k_mid, q_mid, k_out = hb("k_mid"), hb("q_mid"), hb("k_out")
            o_sq_hi = alias("o_sq_hi", [P, T], F32R)
            k_tok, k_end, q_cum, i_feat = hb("k_tok"), hb("k_end"), hb("q_cum"), hb("i_feat")
            o_sq_lo = alias("o_sq_lo", [P, T], F32R)
            i_tok = hb("i_tok")
            qry, keep = hb("qry"), hb("keep")
            scores = hb("scores", (P, NSC, P))
            state = hb("state", (P, NSC, P))
        merged = alias("merged", [P, KC, T])
        merged_lo = alias("merged_lo", [P, KC, T], F32R)
        squares = alias("squares", [P, KC, T])
        act_lo = sb("act_lo", [P, KC, T], F32R)
        act_hi = h_hi
        o_hi = alias("o_hi", [P, KC, T], F32R)
        a_lo = alias("a_lo", [P, KC, T], F32R)
        with ExitStack() as late:
            sb("_a_lo_0_to_4", [P, 5, T], F32, late)
            b_bcast = sb("b_bcast", [P, KC, P], F32, late)
            sb("_a_lo_6", [P, T], F32, late)
            mix_bias = sb("mix_bias", [P, KC, P], F32, late)
        ffn_hi = sb("ffn_hi", [P, KC, T], F32R)

        proj = [ctx.enter_context(nc.psum_tensor(f"proj{i}", [P, T], F32)) for i in range(2)]
        ps_a = ctx.enter_context(nc.psum_tensor("ps_a", [P, T], F32))
        ps_b = ctx.enter_context(nc.psum_tensor("ps_b", [P, T], F32))

        w_loaded = [sem(f"w_loaded{i}") for i in range(2)]
        w_hi_ready, w_lo_ready = sem("w_hi_ready"), sem("w_lo_ready")
        proj_done = sem("proj_done")
        x_loaded = [sem(f"x_loaded{i}") for i in range(KC)]
        x_again = [sem(f"x_again{i}") for i in range(KC)]
        vec_loaded, wsp_loaded, bsp_loaded = sem("vec_loaded"), sem("wsp_loaded"), sem("bsp_loaded")
        out_stored = sem("out_stored")
        pool_const = sem("pool_const")
        lb_exp, lb_step = sem("lb_exp"), sem("lb_step")
        const_ready, rowsum_done, bias_ready = sem("const_ready"), sem("rowsum_done"), sem("bias_ready")
        ones_rounded = sem("ones_rounded")
        sq_ready, sq_pool, ssq_first, ssq_step, ssq_done = (
            sem("sq_ready"), sem("sq_pool"), sem("ssq_first"), sem("ssq_step"), sem("ssq_done"))
        ve_ready, r0_ready = sem("ve_ready"), sem("r0_ready")
        newton, rms_ready = sem("newton"), sem("rms_ready")
        ffn_hi_ready, ffn_lo_ready = sem("ffn_hi_ready"), sem("ffn_lo_ready")
        f_scaled, g_scaled, gb_scaled, u_scaled, ga_scaled, ff_scaled = (
            sem("f_scaled"), sem("g_scaled"), sem("gb_scaled"), sem("u_scaled"), sem("ga_scaled"), sem("ff_scaled"))
        h_hi_ready, h_lo_ready = sem("h_hi_ready"), sem("h_lo_ready")
        sig_ready, f_ready, key_ready, logf_ready, cum_ready = (
            sem("sig_ready"), sem("f_ready"), sem("key_ready"), sem("logf_ready"), sem("cum_ready"))
        mid_ready, last_ready = sem("mid_ready"), sem("last_ready")
        qry_ready, dec_ready, dec2_ready = sem("qry_ready"), sem("dec_ready"), sem("dec2_ready")
        exp_mid, exp_out = sem("exp_mid"), sem("exp_out")
        k_mid_ready, q_mid_ready = sem("k_mid_ready"), sem("q_mid_ready")
        k_end_ready, q_cum_ready = sem("k_end_ready"), sem("q_cum_ready")
        k_out_ready, q_sc_ready = sem("k_out_ready"), sem("q_sc_ready")
        i_feat_ready, i_tok_ready, k_tok_ready = sem("i_feat_ready"), sem("i_tok_ready"), sem("k_tok_ready")
        i_turned, k_turned = sem("i_turned"), sem("k_turned")
        ds_done, state_step = sem("ds_done"), sem("state_step")
        diag_done, cross_done, diag_ready, cross_ready = (
            sem("diag_done"), sem("cross_done"), sem("diag_ready"), sem("cross_ready"))
        o_done, osq_ready, osum_done = sem("o_done"), sem("osq_ready"), sem("osum_done")
        osq_hi_ready, osq_lo_ready = sem("osq_hi_ready"), sem("osq_lo_ready")
        gate_ready, ob_ready, o_ready = sem("gate_ready"), sem("ob_ready"), sem("o_ready")
        ove_ready, or0_ready, onewton = sem("ove_ready"), sem("or0_ready"), sem("onewton")
        o_hi_ready, o_lo_ready = sem("o_hi_ready"), sem("o_lo_ready")
        gate_b_ready, part_ready = sem("gate_b_ready"), sem("part_ready")
        rms_turned, rms_tok_ready = sem("rms_turned"), sem("rms_tok_ready")
        v_done, v_tok_ready = sem("v_done"), sem("v_tok_ready")
        z_centred = sem("z_centred")
        stat_step, ln_r0_ready, bn_step = sem("stat_step"), sem("ln_r0_ready"), sem("bn_step")
        ug_ready, z_ready, mixed_done = sem("ug_ready"), sem("z_ready"), sem("mixed_done")
        mix_ready, a_raw_ready, a_hi_ready, a_lo_ready = (
            sem("mix_ready"), sem("a_raw_ready"), sem("a_hi_ready"), sem("a_lo_ready"))
        gate_a_ready, ya_ready, m_ready = sem("gate_a_ready"), sem("ya_ready"), sem("m_ready")
        m_hi_ready, m_lo_ready = sem("m_hi_ready"), sem("m_lo_ready")
        x1_ready, x1_sq = sem("x1_ready"), sem("x1_sq")
        silu_scaled = sem("silu_scaled")
        silu_ready, act_raw, act_hi_ready, act_lo_ready = (
            sem("silu_ready"), sem("act_raw"), sem("act_hi_ready"), sem("act_lo_ready"))
        down_ready = sem("down_ready")
        tail_done = sem("tail_done")
        out_ready = sem("out_ready")

        block = ctx.enter_context(nc.Block())

        def f32(ap):
            return ap.bitcast(F32)

        def chunks(t2d):
            return t2d.rearrange("p (c t) -> p c t", t=CH)

        def later(k):
            return not isinstance(k, int) or k > 0

        def stepped(engine, count, body):
            body(0)
            with engine.Fori(1, count) as k:
                body(k)

        halves = [slice(0, H), slice(H, T)]

        def supers(t2d):
            return t2d.rearrange("p (c t) -> p c t", t=P)

        tail_tokens = [slice(0, H), slice(H, H + H // 2), slice(H + H // 2, T)]
        last_parts = PARTS[-1]
        n_tail = N_PART[-1] + 2 * last_parts

        def v_bank(t):
            return [proj[0], proj[1], ps_a, ps_b][t // 2][:, t % 2 * H:t % 2 * H + H]

        def tail_weight(c):
            if c < 2:
                return w_hi[c][:, 0:last_parts, :], w_lo[c][:, 0:last_parts, :]
            return tuple(t[:, c - 2, 0:last_parts * P].rearrange("p (k n) -> p k n", n=P) for t in (ffn_hi, h_lo))

        def tail_bank(q, s):
            return proj[q // 2 % 2][:, q % 2 * H:q % 2 * H + (s.stop - s.start)]

        act_before = [sum(PARTS[:i]) for i in range(len(PARTS))]

        @block.sync
        def _(sp):
            sp.dma_start(vecs[:], vectors).then_inc(vec_loaded, 16)
            for c in range(KC):
                sp.dma_start(x_in[:, c, :], x_t[:, c, :]).then_inc(x_loaded[c], 16)
                if c in (0, 3):
                    sp.dma_start(w_raw[c // 3][:], w_stream[c // 3]).then_inc(w_loaded[c // 3], 16)
            with sp.Fori(1, N_BLOCKS // 2) as pair:
                for i in range(2):
                    sp.wait_ge(w_lo_ready, 2 * pair + (i - 1))
                    sp.dma_start(w_raw[i][:], w_stream[2 * pair + i]).then_inc(w_loaded[i], 16)
            for part, s in enumerate(tail_tokens):
                for c in range(KC):
                    sp.wait_ge(out_ready, KC * part + c + 1)
                    sp.dma_start(out_t[:, c, s], resid[:, c, s]).then_inc(out_stored, 16)
            sp.wait_ge(out_stored, 16 * KC * len(tail_tokens))

        @block.gpsimd
        def _(pool):
            nc.gpsimd.memset(ones[:], 1.0).then_inc(const_ready, 1)
            nc.gpsimd.memset(ident[:], 0.0).then_inc(pool_const, 1)
            nc.gpsimd.memset(causal[:], 1.0).then_inc(pool_const, 1)
            pool.wait_ge(pool_const, 2)
            nc.gpsimd.affine_select(out=ident[:], in_=ident[:], compare_op=ALU.not_equal, fill=1.0, base=0,
                                    pattern=[[1, P]], channel_multiplier=-1).then_inc(const_ready, 1)
            nc.gpsimd.affine_select(out=causal[:], in_=causal[:], compare_op=ALU.is_ge, fill=0.0, base=0,
                                    pattern=[[1, P]], channel_multiplier=-1).then_inc(pool_const, 1)
            pool.wait_ge(pool_const, 3)
            nc.gpsimd.memset(causal[0:CH, CH:P], 0.0).then_inc(const_ready, 1)
            for c in range(POOL_SQUARES):
                pool.wait_ge(x_loaded[c], 16)
                nc.gpsimd.tensor_tensor(squares[:, c, :], x_in[:, c, :], x_in[:, c, :], ALU.mult).then_inc(sq_pool, 1)
            for c in range(1, POOL_SQUARES):
                pool.wait_ge(sq_pool, POOL_SQUARES + c - 1)
                nc.gpsimd.tensor_tensor(squares[:, 0, :], squares[:, 0, :], squares[:, c, :], ALU.add
                                        ).then_inc(sq_pool, 1)
            pool.dma_start(spatial_t[:], w_spatial).then_inc(wsp_loaded, 16)
            pool.wait_ge(wsp_loaded, 16)
            nc.gpsimd.affine_select(out=spatial_t[:], in_=spatial_t[:], compare_op=ALU.is_ge, fill=0.0, base=0,
                                    pattern=[[0, KC], [1, P]], channel_multiplier=-1).then_inc(const_ready, 1)
            pool.wait_ge(proj_done, 2 * N_V)
            pool.dma_start(b_bcast[:].rearrange("p g t -> p (g t)"),
                           b_spatial.broadcast_to([P, KC * P])).then_inc(bsp_loaded, 16)
            pool.wait_ge(proj_done, 2 * N_MERGE)
            for c in range(KC):
                pool.dma_start(resid[:, c, :], x_t[:, c, :]).then_inc(x_again[c], 16)

        @block.scalar
        def _(act):
            def split_hi(n, i):
                act.wait_ge(w_loaded[i], 8 * (n - i) + 16)
                if not isinstance(n, int) or n >= 2:
                    act.wait_ge(proj_done, 2 * n - 2)
                nc.scalar.copy(w_hi[i][:], w_raw[i][:]).then_inc(w_hi_ready, 1)

            def rms_guess(s, count):
                act.wait_ge(ve_ready, count)
                nc.scalar.activation(inv_rms[:, s], work[0][:, s], ACT.Abs_reciprocal_sqrt).then_inc(r0_ready, 1)

            act.wait_ge(const_ready, 1)
            nc.scalar.copy(ones_r[:], ones[:]).then_inc(ones_rounded, 1)
            act.wait_ge(vec_loaded, 16)
            for c in range(KC):
                act.wait_ge(x_loaded[c], 16)
                nc.scalar.activation(h_hi[:, c, :], x_in[:, c, :], ACT.Copy,
                                     scale=vecs[:, V_MIX, c:c + 1]).then_inc(h_hi_ready, 1)
                if c == 0:
                    split_hi(0, 0)
                if c == 2:
                    act.wait_ge(lb_step, 3)
                    nc.scalar.activation(lb_tmp[:, 1:3, :], lb_tmp[:, 1:3, :], ACT.Exp).then_inc(lb_exp, 1)
                if c == 3:
                    split_hi(1, 1)
                for q in range(POOL_SQUARES, KC):
                    if c == min(q + 1, KC - 1):
                        nc.scalar.activation(squares[:, q, :], x_in[:, q, :], ACT.Square).then_inc(sq_ready, 1)
            split_hi(2, 0)
            rms_guess(slice(0, T), 1)
            split_hi(3, 1)

            def gate_b(c):
                act.wait_ge(gb_scaled, c + 1)
                nc.scalar.activation(merged[:, c, :], merged[:, c, :], ACT.Sigmoid).then_inc(gate_b_ready, 1)

            def head(h, own=True):
                n = 4 * h
                small = later(h)
                if later(h):
                    split_hi(n + 1, 1)
                if small:
                    split_hi(n + 2, 0)
                if own:
                    act.wait_ge(f_scaled, h + 1)
                    nc.scalar.activation(fgt[:], fgt[:], ACT.Sigmoid).then_inc(sig_ready, 1)
                    act.wait_ge(key_ready, h + 1)
                    nc.scalar.activation(fgt[:], fgt[:], ACT.Ln).then_inc(logf_ready, 1)
                else:
                    gate_b(0)
                if own:
                    act.wait_ge(last_ready, h + 1)
                    if small:
                        act.wait_ge(q_sc_ready, 2 * h)
                    nc.scalar.activation(dec[:], chunks(cum[:])[:, :, CH - 1], ACT.Exp).then_inc(dec_ready, 1)
                    if small:
                        act.wait_ge(diag_done, h)
                    nc.scalar.activation(k_mid[:], fgt[:], ACT.Exp, scale=-1.0).then_inc(exp_mid, 1)
                    nc.scalar.activation(q_mid[:], fgt[:], ACT.Exp).then_inc(exp_mid, 1)
                else:
                    gate_b(1)
                if small:
                    split_hi(n + 3, 1)
                if own:
                    if small:
                        act.wait_ge(cross_done, h)
                        act.wait_ge(k_out_ready, 2 * h)
                    nc.scalar.activation(k_end[:], to_last[:], ACT.Exp).then_inc(exp_out, 1)
                    nc.scalar.activation(q_cum[:], cum[:], ACT.Exp).then_inc(exp_out, 1)
                else:
                    gate_b(2)
                if small:
                    act.wait_ge(o_done, h)
                    if not isinstance(h, int) or h >= 2:
                        act.wait_ge(o_ready, h - 1)
                    nc.scalar.activation(o_sq[:], ps_b[:], ACT.Square).then_inc(osq_ready, 1)
                    act.wait_ge(osq_ready, h)
                    nc.scalar.copy(o_sq_hi[:], o_sq[:]).then_inc(osq_hi_ready, 1)
                split_hi(n + 4, 0)
                if small:
                    act.wait_ge(ove_ready, h)
                    nc.scalar.activation(k_tok[:], o_sq[:], ACT.Abs_reciprocal_sqrt).then_inc(or0_ready, 1)
                if own:
                    act.wait_ge(g_scaled, h + 1)
                    nc.scalar.activation(s_gate[:], s_gate[:], ACT.Silu).then_inc(gate_ready, 1)
                else:
                    gate_b(3)

            head(0)
            head(1)
            with act.Fori(2, HEADS) as h:
                head(h)
            act.wait_ge(q_sc_ready, 2 * HEADS)
            head(HEADS, own=False)

            act.wait_ge(o_ready, HEADS)
            for k in range(4):
                split_hi(N_GATE_B + 5 + k, 1 - k % 2)
                for j in range(2):
                    nc.scalar.copy(o_hi[:, 2 * k + j, :], o_raw[:, 2 * k + j, :]).then_inc(o_hi_ready, 1)
                gate_b(4 + k)
            with act.Fori(0, KC // 2) as k:
                for i in range(2):
                    split_hi(2 * k + (N_OUT_B + 1 + i), 1 - i)

            for f in range(2):
                for b in range(4):
                    split_hi(N_V + 4 * f + b + 1, 1 - b % 2)
                if f == 0:
                    act.wait_ge(rms_tok_ready, 1)
                for t in range(NSC):
                    if t < NSC - 1:
                        act.wait_ge(v_done, (NSC - 1) * f + t + 1)
                    else:
                        act.wait_ge(proj_done, 2 * (N_V + 4 * f + 4))
                    nc.scalar.activation(v_tok[:, 4 * f:4 * f + 4, t, :], v_bank(t).rearrange("p (g n) -> p g n", n=P),
                                         ACT.Gelu_apprx_tanh, scale=rms_tok[:, t:t + 1]).then_inc(v_tok_ready, 1)

            def copy_a(g):
                act.wait_ge(a_raw_ready, g + 1)
                nc.scalar.copy(a_hi[:, g, :], work[1][:]).then_inc(a_hi_ready, 1)

            def u_pair(k):
                for i in range(2):
                    g = 2 * k + i
                    split_hi(g + (N_U + 1), 1 - i)
                    if i or later(k):
                        copy_a(g - 1)
                    else:
                        act.wait_ge(stat_step, 1)
                        nc.scalar.activation(ln_r[:], ln_ve[:], ACT.Abs_reciprocal_sqrt).then_inc(ln_r0_ready, 1)
                    act.wait_ge(u_scaled, g + 1)
                    nc.scalar.activation(work[0][:], work[0][:], ACT.Gelu_apprx_tanh).then_inc(ug_ready, 1)
            stepped(act, KC // 2, u_pair)

            def a_step(j):
                split_hi(2 * j + (N_GATE_A + 1), 1)
                if not later(j):
                    copy_a(KC - 1)
                act.wait_ge(ga_scaled, j + 1)
                nc.scalar.activation(work[2][:], work[2][:], ACT.Sigmoid).then_inc(gate_a_ready, 1)
                split_hi(2 * j + (N_GATE_A + 2), 0)
            stepped(act, KC, a_step)
            for c in range(KC):
                act.wait_ge(m_ready, c + 1)
                nc.scalar.copy(h_hi[:, c, :], merged[:, c, :]).then_inc(m_hi_ready, 1)

            for c in range(KC):
                split_hi(c + (N_MERGE + 1), 1 - c % 2)
                act.wait_ge(x1_ready, c + 1)
                nc.scalar.activation(ffn_hi[:, c, :], resid[:, c, :], ACT.Copy,
                                     scale=vecs[:, V_FFN, c:c + 1]).then_inc(ffn_hi_ready, 1)
                if c:
                    act.wait_ge(ssq_step, c)
                nc.scalar.activation(work[1][:], resid[:, c, :], ACT.Square).then_inc(x1_sq, 1)

            for p, parts in enumerate(PARTS):
                def ff_step(j):
                    n = N_PART[p] + 2 * j
                    k = act_before[p] + j
                    split_hi(n + 1, 1)
                    split_hi(n + 2, 0)
                    if p == 0 and not later(j):
                        rms_guess(slice(0, T), 2)
                    act.wait_ge(ff_scaled, k + 1)
                    nc.scalar.activation(work[0][:], work[0][:], ACT.Silu).then_inc(silu_ready, 1)
                    act.wait_ge(act_raw, k + 1)
                    nc.scalar.copy(act_hi[:, j, :], work[1][:]).then_inc(act_hi_ready, 1)
                stepped(act, parts, ff_step)
                n_down = N_PART[p] + 2 * parts
                if p < len(PARTS) - 1:
                    with act.Fori(0, KC // 2) as k:
                        for i in range(2):
                            split_hi(2 * k + (n_down + 1 + i), 1 - i)
            split_hi(n_tail + 1, 1)
            def tail_hi(c):
                act.wait_ge(w_loaded[c % 2], 8 * (n_tail + c - c % 2) + 16)
                nc.scalar.copy(tail_weight(c)[0], w_raw[c % 2][:, 0:last_parts, :]).then_inc(w_hi_ready, 1)
            for c in range(2, 6):
                tail_hi(c)
            act.wait_ge(act_lo_ready, FC)
            for part, s in enumerate(tail_tokens):
                for c in range(KC):
                    q = KC * part + c
                    act.wait_ge(down_ready, KC * (len(PARTS) - 1) + q + 1)
                    if c:
                        act.wait_ge(ssq_step, KC + (KC - 1) * part + c)
                    nc.scalar.activation(work[1][:, s], resid[:, c, s], ACT.Square).then_inc(x1_sq, 1)
                    if q < 2:
                        tail_hi(6 + q)
                    if part and c == 1:
                        rms_guess(tail_tokens[part - 1], 2 + part)
            rms_guess(tail_tokens[-1], 2 + len(tail_tokens))

        @block.vector
        def _(dve):
            def split_lo(n, i):
                dve.wait_ge(w_hi_ready, n + 1)
                if not isinstance(n, int) or n >= 2:
                    dve.wait_ge(proj_done, 2 * n - 2)
                nc.vector.tensor_tensor(w_lo[i][:], w_raw[i][:], f32(w_hi[i][:]), ALU.subtract
                                        ).then_inc(w_lo_ready, 1)

            def inverse_rms(s, count, between=None):
                dve.wait_ge(ssq_done, count)
                nc.vector.tensor_scalar(work[0][:, s], ps_a[:, s], 1.0 / D, EPS, ALU.mult, ALU.add
                                        ).then_inc(ve_ready, 1)
                if between is not None:
                    between()
                dve.wait_ge(r0_ready, count)
                nc.vector.tensor_tensor(work[2][:, s], inv_rms[:, s], inv_rms[:, s], ALU.mult).then_inc(newton, 1)
                dve.wait_ge(newton, 2 * count - 1)
                nc.vector.scalar_tensor_tensor(out=work[2][:, s], in0=work[0][:, s], scalar=-0.5, in1=work[2][:, s],
                                               op0=ALU.mult, op1=ALU.mult).then_inc(newton, 1)
                dve.wait_ge(newton, 2 * count)
                nc.vector.scalar_tensor_tensor(out=inv_rms[:, s], in0=work[2][:, s], scalar=1.5, in1=inv_rms[:, s],
                                               op0=ALU.add, op1=ALU.mult).then_inc(rms_ready, 1)
                dve.wait_ge(rms_ready, count)

            def times_inv_rms(out, ps, scaled):
                nc.vector.tensor_tensor(out, ps[:], inv_rms[:], ALU.mult).then_inc(scaled, 1)

            nc.vector.memset(keep[:], 1.0).then_inc(lb_step, 1)
            nc.vector.memset(scores[:], 0.0).then_inc(lb_step, 1)
            dve.wait_ge(vec_loaded, 16)
            dve.wait_ge(lb_step, 2)
            nc.vector.memset(chunks(keep[:])[:, :, 0:1], 0.0)
            nc.vector.tensor_tensor(lb_tmp[:, 0, :], vecs[:, V_LB0, :], vecs[:, V_LB1, :], ALU.max).then_inc(lb_exp, 1)
            dve.wait_ge(lb_exp, 1)
            nc.vector.tensor_tensor(lb_tmp[:, 1:3, :], vecs[:, V_LB0:V_LB1 + 1, :],
                                    lb_tmp[:, 0:1, :].broadcast_to([P, 2, KC]), ALU.subtract).then_inc(lb_step, 1)

            def add_squares(c):
                dve.wait_ge(sq_ready, c - POOL_SQUARES + 1)
                if c > POOL_SQUARES + 1:
                    dve.wait_ge(ssq_first, c - POOL_SQUARES - 1)
                nc.vector.tensor_tensor(squares[:, POOL_SQUARES, :], squares[:, POOL_SQUARES, :],
                                        squares[:, c, :], ALU.add).then_inc(ssq_first, 1)
            for c in range(KC):
                dve.wait_ge(h_hi_ready, c + 1)
                nc.vector.scalar_tensor_tensor(out=h_lo[:, c, :], in0=x_in[:, c, :], scalar=vecs[:, V_MIX, c:c + 1],
                                               in1=f32(h_hi[:, c, :]), op0=ALU.mult, op1=ALU.subtract
                                               ).then_inc(h_lo_ready, 1)
                if c == 0:
                    split_lo(0, 0)
                if c == 3:
                    split_lo(1, 1)
                if c - 1 > POOL_SQUARES + 1:
                    add_squares(c - 2)
            add_squares(KC - 2)
            add_squares(KC - 1)
            dve.wait_ge(sq_pool, 2 * POOL_SQUARES - 1)
            dve.wait_ge(ssq_first, KC - POOL_SQUARES - 1)
            nc.vector.tensor_tensor(squares[:, 0, :], squares[:, 0, :], squares[:, POOL_SQUARES, :], ALU.add
                                    ).then_inc(ssq_first, 1)
            dve.wait_ge(lb_exp, 2)
            nc.vector.tensor_tensor(lb_tmp[:, 3, :], lb_tmp[:, 1, :], lb_tmp[:, 2, :], ALU.add).then_inc(lb_step, 1)
            dve.wait_ge(lb_step, 4)
            nc.vector.reciprocal(lb_tmp[:, 3, :], lb_tmp[:, 3, :]).then_inc(lb_step, 1)
            dve.wait_ge(lb_step, 5)
            nc.vector.tensor_tensor(lb[:], lb_tmp[:, 1, :], lb_tmp[:, 3, :], ALU.mult).then_inc(lb_step, 1)
            dve.wait_ge(lb_step, 6)
            nc.vector.tensor_scalar(one_minus_lb[:], lb[:], -1.0, 1.0, ALU.mult, ALU.add).then_inc(lb_step, 1)
            dve.wait_ge(lb_step, 7)
            inverse_rms(slice(0, T), 1, between=lambda: split_lo(2, 0))

            def take_query(h):
                dve.wait_ge(proj_done, 8 * h + 4)
                nc.vector.scalar_tensor_tensor(out=qry[:], in0=proj[1][:], scalar=DK_SCALE, in1=inv_rms[:],
                                               op0=ALU.mult, op1=ALU.mult).then_inc(qry_ready, 1)

            def head(h, own=True):
                n = 4 * h
                small = later(h)
                if small:
                    split_lo(n + 1, 1)
                if small:
                    dve.wait_ge(i_turned, h)
                    if not isinstance(h, int) or h >= 2:
                        dve.wait_ge(o_ready, h - 1)
                    nc.vector.tensor_copy(i_tok[:], ps_a[:]).then_inc(i_tok_ready, 1)
                dve.wait_ge(proj_done, 2 * n + 2)
                if own:
                    if small:
                        dve.wait_ge(exp_mid, 2 * h)
                    times_inv_rms(fgt[:], proj[0], f_scaled)
                else:
                    times_inv_rms(merged[:, 0, :], proj[0], gb_scaled)
                if small:
                    split_lo(n + 2, 0)
                else:
                    take_query(h)
                    split_lo(n + 3, 1)
                if small:
                    dve.wait_ge(k_turned, h)
                    nc.vector.tensor_copy(k_tok[:, 0:T - P], ps_b[:, 0:T - P]).then_inc(k_tok_ready, 1)
                if own:
                    dve.wait_ge(sig_ready, h + 1)
                    nc.vector.tensor_scalar(fgt[:], fgt[:], one_minus_lb[:, bass.ds(h, 1)], lb[:, bass.ds(h, 1)],
                                            ALU.mult, ALU.add).then_inc(f_ready, 1)
                    dve.wait_ge(f_ready, h + 1)
                    nc.vector.tensor_scalar(key[:], fgt[:], -1.0, 1.0, ALU.mult, ALU.add).then_inc(key_ready, 1)
                if own:
                    dve.wait_ge(logf_ready, h + 1)
                    if small:
                        dve.wait_ge(exp_out, 2 * h)
                    nc.vector.tensor_tensor_scan(cum[:], keep[:], fgt[:], 0.0, ALU.mult, ALU.add
                                                 ).then_inc(cum_ready, 1)
                    dve.wait_ge(cum_ready, h + 1)
                    nc.vector.tensor_tensor(chunks(fgt[:]), chunks(cum[:]),
                                            chunks(cum[:])[:, :, CH // 2 - 1:CH // 2].broadcast_to([P, NCH, CH]),
                                            ALU.subtract).then_inc(mid_ready, 1)
                    nc.vector.tensor_tensor(chunks(to_last[:]),
                                            chunks(cum[:])[:, :, CH - 1:CH].broadcast_to([P, NCH, CH]),
                                            chunks(cum[:]), ALU.subtract).then_inc(last_ready, 1)
                if small:
                    dve.wait_ge(dec2_ready, h)
                    dve.wait_ge(ds_done, h)
                    if not isinstance(h, int) or h >= 2:
                        dve.wait_ge(o_done, h - 1)
                    ds = supers(ps_a[:])
                    nc.vector.tensor_copy(state[:, 0, :], ds[:, 0, :]).then_inc(state_step, 1)
                    for c in range(1, NSC - 1):
                        dve.wait_ge(state_step, (NSC - 1) * (h - 1) + c)
                        nc.vector.scalar_tensor_tensor(out=state[:, c, :], in0=state[:, c - 1, :],
                                                       scalar=dec2[:, c:c + 1], in1=ds[:, c, :],
                                                       op0=ALU.mult, op1=ALU.add).then_inc(state_step, 1)
                if own and small:
                    dve.wait_ge(q_cum_ready, h)
                    take_query(h)
                elif not own:
                    dve.wait_ge(proj_done, 2 * n + 4)
                    times_inv_rms(merged[:, 1, :], proj[1], gb_scaled)
                if small:
                    dve.wait_ge(const_ready, 3)
                    dve.wait_ge(diag_done, h)
                    nc.vector.copy_predicated(scores[:], causal[:].bitcast(I32)[:, None, :].broadcast_to([P, NSC, P]),
                                              supers(ps_b[:])).then_inc(diag_ready, 1)
                if small:
                    split_lo(n + 3, 1)
                if own:
                    dve.wait_ge(exp_mid, 2 * h + 1)
                    nc.vector.tensor_tensor(k_mid[:], k_mid[:], key[:], ALU.mult).then_inc(k_mid_ready, 1)
                    dve.wait_ge(exp_mid, 2 * h + 2)
                    dve.wait_ge(qry_ready, h + 1)
                    nc.vector.tensor_tensor(q_mid[:], q_mid[:], qry[:], ALU.mult).then_inc(q_mid_ready, 1)
                if small:
                    dve.wait_ge(cross_done, h)
                    dve.wait_ge(diag_ready, h)
                    nc.vector.tensor_copy(scores[0:CH, :, CH:P],
                                          ps_a[0:CH, 0:H].rearrange("p (c t) -> p c t", t=CH)
                                          ).then_inc(cross_ready, 1)
                dve.wait_ge(proj_done, 2 * n + 6)
                if own:
                    if small:
                        dve.wait_ge(i_turned, h)
                    times_inv_rms(i_feat[:], proj[0] if small else ps_b, i_feat_ready)
                else:
                    times_inv_rms(merged[:, 2, :], proj[0], gb_scaled)
                if small:
                    dve.wait_ge(osq_hi_ready, h)
                    nc.vector.tensor_tensor(o_sq_lo[:], o_sq[:], f32(o_sq_hi[:]), ALU.subtract
                                            ).then_inc(osq_lo_ready, 1)
                split_lo(n + 4, 0)
                if own:
                    dve.wait_ge(exp_out, 2 * h + 1)
                    nc.vector.tensor_tensor(k_end[:], k_end[:], key[:], ALU.mult).then_inc(k_end_ready, 1)
                    dve.wait_ge(exp_out, 2 * h + 2)
                    nc.vector.tensor_tensor(q_cum[:], q_cum[:], qry[:], ALU.mult).then_inc(q_cum_ready, 1)
                    dve.wait_ge(dec_ready, h + 1)
                    d = dec[:].rearrange("p (c two) -> p c two", two=2)
                    ke = k_end[:].rearrange("p (c two t) -> p c two t", two=2, t=CH)
                    ko = k_out[:].rearrange("p (c two t) -> p c two t", two=2, t=CH)
                    qc = q_cum[:].rearrange("p (c two t) -> p c two t", two=2, t=CH)
                    qs = q_sc[:].rearrange("p (c two t) -> p c two t", two=2, t=CH)
                    if small:
                        dve.wait_ge(k_turned, h)
                    dve.wait_ge(k_end_ready, h + 1)
                    nc.vector.tensor_tensor(ko[:, :, 0, :], ke[:, :, 0, :],
                                            d[:, :, 1:2].broadcast_to([P, NSC, CH]), ALU.mult).then_inc(k_out_ready, 1)
                    nc.vector.tensor_copy(ko[:, :, 1, :], ke[:, :, 1, :]).then_inc(k_out_ready, 1)
                    if small:
                        dve.wait_ge(o_done, h)
                    dve.wait_ge(q_cum_ready, h + 1)
                    nc.vector.tensor_tensor(qs[:, :, 1, :], qc[:, :, 1, :],
                                            d[:, :, 0:1].broadcast_to([P, NSC, CH]), ALU.mult).then_inc(q_sc_ready, 1)
                    nc.vector.tensor_tensor(dec2[:], d[:, :, 0], d[:, :, 1], ALU.mult).then_inc(dec2_ready, 1)
                    nc.vector.tensor_copy(qs[:, :, 0, :], qc[:, :, 0, :]).then_inc(q_sc_ready, 1)
                if small:
                    dve.wait_ge(osq_ready, h)
                    dve.wait_ge(gate_ready, h)
                    nc.vector.scalar_tensor_tensor(out=o_raw[:, h - 1, :], in0=ps_b[:],
                                                   scalar=vecs[:, V_HG, bass.ds(h - 1, 1)], in1=s_gate[:],
                                                   op0=ALU.mult, op1=ALU.mult).then_inc(ob_ready, 1)
                    dve.wait_ge(osum_done, h)
                    nc.vector.tensor_scalar(o_sq[:], ps_a[:], 1.0 / P, EPS, ALU.mult, ALU.add).then_inc(ove_ready, 1)
                    dve.wait_ge(or0_ready, h)
                    nc.vector.tensor_tensor(i_tok[:], k_tok[:], k_tok[:], ALU.mult).then_inc(onewton, 1)
                    dve.wait_ge(onewton, 3 * h - 2)
                    nc.vector.scalar_tensor_tensor(out=i_tok[:], in0=o_sq[:], scalar=-0.5, in1=i_tok[:],
                                                   op0=ALU.mult, op1=ALU.mult).then_inc(onewton, 1)
                    dve.wait_ge(onewton, 3 * h - 1)
                    nc.vector.scalar_tensor_tensor(out=k_tok[:], in0=i_tok[:], scalar=1.5, in1=k_tok[:],
                                                   op0=ALU.add, op1=ALU.mult).then_inc(onewton, 1)
                    dve.wait_ge(onewton, 3 * h)
                    nc.vector.tensor_tensor(o_raw[:, h - 1, :], o_raw[:, h - 1, :], k_tok[:], ALU.mult
                                            ).then_inc(o_ready, 1)
                dve.wait_ge(proj_done, 2 * n + 8)
                if own:
                    times_inv_rms(s_gate[:], proj[1], g_scaled)
                else:
                    times_inv_rms(merged[:, 3, :], proj[1], gb_scaled)

            head(0)
            head(1)
            with dve.Fori(2, HEADS) as h:
                head(h)
            head(HEADS, own=False)

            with dve.Fori(0, 2) as k:
                for i in range(2):
                    split_lo(2 * k + (N_GATE_B + 5 + i), 1 - i)
                    for j in range(2):
                        c = 4 * k + (2 * i + j)
                        dve.wait_ge(o_hi_ready, c + 1)
                        nc.vector.tensor_tensor(o_lo[:, c, :], o_raw[:, c, :], f32(o_hi[:, c, :]), ALU.subtract
                                                ).then_inc(o_lo_ready, 1)
                    dve.wait_ge(proj_done, 4 * k + (2 * (N_GATE_B + 4 + i) + 2))
                    times_inv_rms(merged[:, 2 * k + (4 + i), :], proj[i], gb_scaled)
            dve.wait_ge(rms_turned, 1)
            nc.vector.tensor_copy(rms_tok[:], ps_a[:, 0:NSC]).then_inc(rms_tok_ready, 1)
            with dve.Fori(0, KC // 2) as k:
                for i in range(2):
                    split_lo(2 * k + (N_OUT_B + 1 + i), 1 - i)
                    dve.wait_ge(proj_done, 4 * k + (2 * (N_OUT_B + i) + 2))
                    dve.wait_ge(gate_b_ready, 2 * k + (i + 1))
                    nc.vector.tensor_tensor(merged[:, 2 * k + i, :], proj[i][:], merged[:, 2 * k + i, :], ALU.mult
                                            ).then_inc(part_ready, 1)

            def group_stats(part):
                for t in range(NSC):
                    dve.wait_ge(v_tok_ready, NSC * part + t + 1)
                    nc.vector.bn_stats(stats[:, t, part, :], v_tok[:, 4 * part:4 * part + 4, t, :]
                                       ).then_inc(bn_step, 1)

            for j in range(KC):
                split_lo(N_V + 1 + j, 1 - j % 2)
                if j == 4:
                    group_stats(0)

            def mixing_bias():
                dve.wait_ge(rowsum_done, 1)
                dve.wait_ge(bsp_loaded, 16)
                for g in range(KC):
                    nc.vector.scalar_tensor_tensor(out=mix_bias[:, g, :], in0=supers(ps_b[:])[:, g, :],
                                                   scalar=vecs[:, V_LNB, g:g + 1], in1=b_bcast[:, g, :],
                                                   op0=ALU.mult, op1=ALU.add).then_inc(bias_ready, 1)
                dve.wait_ge(bias_ready, KC)

            def mix(g, ps):
                dve.wait_ge(mixed_done, g + 1)
                if later(g):
                    dve.wait_ge(a_hi_ready, g)
                nc.vector.scalar_tensor_tensor(
                    out=supers(work[1][:]), in0=supers(ps[:]), scalar=vecs[:, V_LNG, bass.ds(g, 1)],
                    in1=mix_bias[:, g, :][:, None, :].broadcast_to([P, NSC, P]) if isinstance(g, int)
                    else mix_bias[:, bass.ds(g, 1), :].broadcast_to([P, NSC, P]),
                    op0=ALU.mult, op1=ALU.add).then_inc(mix_ready, 1)
                dve.wait_ge(mix_ready, g + 1)
                dve.wait_ge(ug_ready, g + 1)
                nc.vector.tensor_tensor(work[1][:], work[1][:], work[0][:], ALU.mult).then_inc(a_raw_ready, 1)
                dve.wait_ge(a_hi_ready, g + 1)
                nc.vector.tensor_tensor(a_lo[:, g, :], work[1][:], f32(a_hi[:, g, :]), ALU.subtract
                                        ).then_inc(a_lo_ready, 1)

            def layer_norm_stats():
                group_stats(1)
                dve.wait_ge(bn_step, 2 * NSC)
                for t in range(NSC):
                    nc.vector.bn_aggr(mean_var[:, t, :], stats[:, t, :, :].rearrange("p a b -> p (a b)")
                                      ).then_inc(bn_step, 1)
                dve.wait_ge(bn_step, 3 * NSC)
                nc.vector.tensor_scalar(ln_ve[:], mean_var[:, :, 1], EPS, None, ALU.add).then_inc(stat_step, 1)
                dve.wait_ge(ln_r0_ready, 1)
                nc.vector.tensor_tensor(ln_t[:], ln_r[:], ln_r[:], ALU.mult).then_inc(stat_step, 1)
                dve.wait_ge(stat_step, 2)
                nc.vector.scalar_tensor_tensor(out=ln_t[:], in0=ln_ve[:], scalar=-0.5, in1=ln_t[:],
                                               op0=ALU.mult, op1=ALU.mult).then_inc(stat_step, 1)
                dve.wait_ge(stat_step, 3)
                nc.vector.scalar_tensor_tensor(out=ln_r[:], in0=ln_t[:], scalar=1.5, in1=ln_r[:],
                                               op0=ALU.add, op1=ALU.mult).then_inc(stat_step, 1)
                dve.wait_ge(stat_step, 4)

            def u_pair(k):
                for i in range(2):
                    g = 2 * k + i
                    split_lo(g + (N_U + 1), 1 - i)
                    if i or later(k):
                        mix(g - 1, [ps_b, ps_a][i])
                    else:
                        layer_norm_stats()
                        mixing_bias()
                    nc.vector.tensor_tensor(supers(work[2][:]), v_tok[:, g, :, :],
                                            mean_var[:, :, 0:1].broadcast_to([P, NSC, P]), ALU.subtract
                                            ).then_inc(z_centred, 1)
                    dve.wait_ge(z_centred, g + 1)
                    nc.vector.tensor_tensor(supers(work[2][:]), supers(work[2][:]),
                                            ln_r[:, :, None].broadcast_to([P, NSC, P]), ALU.mult
                                            ).then_inc(z_ready, 1)
                    dve.wait_ge(proj_done, 2 * g + (2 * N_U + 2))
                    times_inv_rms(work[0][:], proj[i], u_scaled)
            stepped(dve, KC // 2, u_pair)

            def a_step(j):
                split_lo(2 * j + (N_GATE_A + 1), 1)
                if not later(j):
                    mix(KC - 1, ps_b)
                dve.wait_ge(proj_done, 4 * j + (2 * N_GATE_A + 2))
                times_inv_rms(work[2][:], proj[0], ga_scaled)
                split_lo(2 * j + (N_GATE_A + 2), 0)
                if isinstance(j, int) and j == KC - 1:
                    for c in range(KC - 1):
                        merged_low(c)
                dve.wait_ge(proj_done, 4 * j + (2 * N_GATE_A + 4))
                dve.wait_ge(gate_a_ready, j + 1)
                nc.vector.tensor_tensor(work[0][:], proj[1][:], work[2][:], ALU.mult).then_inc(ya_ready, 1)
                dve.wait_ge(ya_ready, j + 1)
                nc.vector.tensor_tensor(merged[:, j, :], merged[:, j, :], work[0][:], ALU.add).then_inc(m_ready, 1)

            def merged_low(c):
                dve.wait_ge(m_hi_ready, c + 1)
                nc.vector.tensor_tensor(merged_lo[:, c, :], merged[:, c, :], f32(h_hi[:, c, :]), ALU.subtract
                                        ).then_inc(m_lo_ready, 1)
            stepped(dve, KC - 1, a_step)
            a_step(KC - 1)
            merged_low(KC - 1)

            for c in range(KC):
                split_lo(N_MERGE + 1 + c, 1 - c % 2)
                dve.wait_ge(proj_done, 2 * (N_MERGE + c) + 2)
                dve.wait_ge(x_again[c], 16)
                nc.vector.tensor_tensor(resid[:, c, :], proj[c % 2][:], resid[:, c, :], ALU.add).then_inc(x1_ready, 1)
                dve.wait_ge(ffn_hi_ready, c + 1)
                nc.vector.scalar_tensor_tensor(out=h_lo[:, c, :], in0=resid[:, c, :], scalar=vecs[:, V_FFN, c:c + 1],
                                               in1=f32(ffn_hi[:, c, :]), op0=ALU.mult, op1=ALU.subtract
                                               ).then_inc(ffn_lo_ready, 1)
                dve.wait_ge(x1_sq, c + 1)
                if c:
                    dve.wait_ge(ssq_step, c)
                    nc.vector.tensor_tensor(work[0][:], work[0][:], work[1][:], ALU.add).then_inc(ssq_step, 1)
                else:
                    nc.vector.tensor_copy(work[0][:], work[1][:]).then_inc(ssq_step, 1)

            for p, parts in enumerate(PARTS):
                def ff_step(j):
                    n = N_PART[p] + 2 * j
                    k = act_before[p] + j
                    split_lo(n + 1, 1)
                    if p == 0 and not later(j):
                        inverse_rms(slice(0, T), 2, between=lambda: split_lo(n + 2, 0))
                    dve.wait_ge(proj_done, 2 * n + 2)
                    times_inv_rms(work[0][:], proj[0], ff_scaled)
                    if p or later(j):
                        split_lo(n + 2, 0)
                    dve.wait_ge(silu_ready, k + 1)
                    nc.vector.tensor_tensor(work[0][:], work[0][:], inv_rms[:], ALU.mult).then_inc(silu_scaled, 1)
                    dve.wait_ge(silu_scaled, k + 1)
                    dve.wait_ge(proj_done, 2 * n + 4)
                    nc.vector.tensor_tensor(work[1][:], proj[1][:], work[0][:], ALU.mult).then_inc(act_raw, 1)
                    dve.wait_ge(act_hi_ready, k + 1)
                    nc.vector.tensor_tensor(act_lo[:, j, :], work[1][:], f32(act_hi[:, j, :]), ALU.subtract
                                            ).then_inc(act_lo_ready, 1)
                stepped(dve, parts, ff_step)
                n_down = N_PART[p] + 2 * parts
                if p < len(PARTS) - 1:
                    with dve.Fori(0, KC // 2) as k:
                        for i in range(2):
                            split_lo(2 * k + (n_down + 1 + i), 1 - i)
                            dve.wait_ge(proj_done, 4 * k + (2 * (n_down + i) + 2))
                            nc.vector.tensor_tensor(resid[:, 2 * k + i, :], proj[i][:], resid[:, 2 * k + i, :], ALU.add
                                                    ).then_inc(down_ready, 1)
            def tail_lo(c):
                dve.wait_ge(w_hi_ready, n_tail + c + 1)
                hi, lo = tail_weight(c)
                nc.vector.tensor_tensor(lo, w_raw[c % 2][:, 0:last_parts, :], f32(hi), ALU.subtract
                                        ).then_inc(w_lo_ready, 1)

            def store_ready(s, c):
                nc.vector.scalar_tensor_tensor(out=resid[:, c, s], in0=resid[:, c, s],
                                               scalar=vecs[:, V_FIN, c:c + 1], in1=inv_rms[:, s],
                                               op0=ALU.mult, op1=ALU.mult).then_inc(out_ready, 1)
            split_lo(n_tail + 1, 1)
            for c in range(2, 4):
                tail_lo(c)
            for part, s in enumerate(tail_tokens):
                for c in range(KC):
                    q = KC * part + c
                    dve.wait_ge(tail_done, q + 1)
                    nc.vector.tensor_tensor(resid[:, c, s], tail_bank(q, s), resid[:, c, s], ALU.add
                                            ).then_inc(down_ready, 1)
                    if part == 0 and c + 4 < KC:
                        tail_lo(c + 4)
                    if c < KC - 1:
                        dve.wait_ge(x1_sq, KC + q + 1)
                        if c:
                            dve.wait_ge(ssq_step, KC + (KC - 1) * part + c)
                            nc.vector.tensor_tensor(work[0][:, s], work[0][:, s], work[1][:, s], ALU.add
                                                    ).then_inc(ssq_step, 1)
                        else:
                            nc.vector.tensor_copy(work[0][:, s], work[1][:, s]).then_inc(ssq_step, 1)
                    if part and c == 1:
                        inverse_rms(tail_tokens[part - 1], 2 + part)
                    if part and 2 <= c < 6:
                        for cc in (2 * c - 4, 2 * c - 3):
                            store_ready(tail_tokens[part - 1], cc)
            inverse_rms(tail_tokens[-1], 2 + len(tail_tokens))
            for c in range(KC):
                store_ready(tail_tokens[-1], c)

        @block.tensor
        def _(pe):
            def products(out, hi, lo, i, k, s, last_k=KC - 1):
                nc.tensor.matmul(out[:, s], w_hi[i][:, k, :], hi[:, k, s], start=(k == 0), stop=False)
                nc.tensor.matmul(out[:, s], w_hi[i][:, k, :], lo[:, k, s], start=False, stop=False)
                return nc.tensor.matmul(out[:, s], w_lo[i][:, k, :], hi[:, k, s], start=False, stop=(k == last_k))

            def wait_block(n, free=None):
                pe.wait_ge(w_hi_ready, n + 1)
                pe.wait_ge(w_lo_ready, n + 1)
                if free is not None:
                    pe.wait_ge(*free)

            def half_block(n, i, half, hi, lo, free=None, chunks_in=KC, between=None, out=None):
                if half == 0:
                    wait_block(n, free)
                for k in range(chunks_in):
                    if between is not None and k == between[0]:
                        between[1]()
                    last = products(out or proj[i], hi, lo, i, k, halves[half], chunks_in - 1)
                last.then_inc(proj_done, 1)

            def full_block(n, i, hi, lo, free=None, chunks_in=KC, wait_chunk=None):
                if wait_chunk is None:
                    half_block(n, i, 0, hi, lo, free=free, chunks_in=chunks_in)
                    half_block(n, i, 1, hi, lo, chunks_in=chunks_in)
                else:
                    wait_block(n, free)
                    for k in range(chunks_in):
                        wait_chunk(k)
                        for s in halves:
                            last = products(proj[i], hi, lo, i, k, s, chunks_in - 1)
                            if k == chunks_in - 1:
                                last.then_inc(proj_done, 1)

            def first_blocks():
                lead = KC // 2
                order = [(0, k) for k in range(lead)]
                order += [(1, 0), (0, 4), (1, 1), (1, 2), (0, 5), (1, 3), (0, 6), (1, 4), (0, 7)]
                order += [(1, k) for k in range(5, KC)]
                wait_block(0)
                for i, k in order:
                    if i == 0:
                        pe.wait_ge(h_hi_ready, k + 1)
                        pe.wait_ge(h_lo_ready, k + 1)
                    elif k == 0:
                        wait_block(1)
                    if (i, k) == (1, 5):
                        pe.wait_ge(const_ready, 1)
                        sum_squares(squares[:, 0, :], ssq_first, KC - POOL_SQUARES)
                    for s in halves:
                        last = products(proj[i], h_hi, h_lo, i, k, s)
                        if k == KC - 1:
                            last.then_inc(proj_done, 1)

            def tail_squares(part):
                s = tail_tokens[part]
                pe.wait_ge(ssq_step, KC + (KC - 1) * (part + 1))
                nc.tensor.matmul(ps_a[:, s], ones[:], work[0][:, s], start=True, stop=False)
                pe.wait_ge(x1_sq, KC + KC * (part + 1))
                nc.tensor.matmul(ps_a[:, s], ones[:], work[1][:, s], start=False, stop=True).then_inc(ssq_done, 1)

            def sum_squares(tile, ready, count):
                pe.wait_ge(ready, count)
                for s in halves:
                    last = nc.tensor.matmul(ps_a[:, s], ones[:], tile[:, s], start=True, stop=True)
                last.then_inc(ssq_done, 1)

            def head(h, own=True):
                n = 4 * h
                small = later(h)
                first = isinstance(h, int) and h == 0

                def slot(b, half):
                    if own:
                        free = [(i_feat_ready, h), (g_scaled, h), (f_scaled, h + 1), (qry_ready, h + 1)][b]
                    else:
                        free = [(i_feat_ready, HEADS), (g_scaled, HEADS), (gb_scaled, 1), (gb_scaled, 2)][b]
                    if first and b < 2:
                        if b == half == 0:
                            first_blocks()
                    elif first and b == 2:
                        half_block(n + b, 0, half, h_hi, h_lo, out=ps_b)
                    else:
                        half_block(n + b, b % 2, half, h_hi, h_lo, free=free)

                slot(0, 0)
                if small:
                    pe.wait_ge(i_feat_ready, h)
                    if not isinstance(h, int) or h >= 2:
                        pe.wait_ge(ove_ready, h - 1)
                    for c in range(NSC):
                        last = nc.tensor.transpose(supers(ps_a[:])[:, c, :], supers(i_feat[:])[:, c, :], ident[:])
                    last.then_inc(i_turned, 1)
                slot(0, 1)
                if small:
                    pe.wait_ge(k_out_ready, 2 * h)
                    if not isinstance(h, int) or h >= 2:
                        pe.wait_ge(ob_ready, h - 1)
                    for c in range(NSC - 1):
                        last = nc.tensor.transpose(supers(ps_b[:])[:, c, :], supers(k_out[:])[:, c, :], ident[:])
                    last.then_inc(k_turned, 1)
                slot(1, 0)
                if small:
                    pe.wait_ge(i_tok_ready, h)
                    pe.wait_ge(k_tok_ready, h)
                    for c in range(NSC - 1):
                        last = nc.tensor.matmul(supers(ps_a[:])[:, c, :], supers(k_tok[:])[:, c, :],
                                                supers(i_tok[:])[:, c, :], start=True, stop=True)
                    last.then_inc(ds_done, 1)
                slot(1, 1)
                if small:
                    pe.wait_ge(k_mid_ready, h)
                    pe.wait_ge(q_mid_ready, h)
                    for c in range(NSC):
                        last = nc.tensor.matmul(supers(ps_b[:])[:, c, :], supers(k_mid[:])[:, c, :],
                                                supers(q_mid[:])[:, c, :], start=True, stop=True)
                    last.then_inc(diag_done, 1)
                slot(2, 0)
                if small:
                    pe.wait_ge(state_step, (NSC - 1) * h)
                    pe.wait_ge(k_end_ready, h)
                    pe.wait_ge(q_cum_ready, h)
                    for c in range(NSC):
                        last = nc.tensor.matmul(ps_a[0:CH, CH * c:CH * c + CH], chunks(k_end[:])[:, 2 * c, :],
                                                chunks(q_cum[:])[:, 2 * c + 1, :], start=True, stop=True)
                    last.then_inc(cross_done, 1)
                slot(2, 1)
                if small:
                    pe.wait_ge(diag_ready, h)
                    pe.wait_ge(cross_ready, h)
                    pe.wait_ge(q_sc_ready, 2 * h)
                    for c in range(NSC):
                        last = nc.tensor.matmul(supers(ps_b[:])[:, c, :], supers(i_tok[:])[:, c, :],
                                                scores[:, c, :], start=True, stop=(c == 0))
                        if c > 0:
                            last = nc.tensor.matmul(supers(ps_b[:])[:, c, :], state[:, c - 1, :],
                                                    supers(q_sc[:])[:, c, :], start=False, stop=True)
                    last.then_inc(o_done, 1)
                slot(3, 0)
                if small:
                    pe.wait_ge(ones_rounded, 1)
                    pe.wait_ge(osq_hi_ready, h)
                    pe.wait_ge(osq_lo_ready, h)
                    for s in halves:
                        nc.tensor.matmul(ps_a[:, s], ones_r[:], o_sq_hi[:, s], start=True, stop=False)
                        last = nc.tensor.matmul(ps_a[:, s], ones_r[:], o_sq_lo[:, s], start=False, stop=True)
                    last.then_inc(osum_done, 1)
                slot(3, 1)

            head(0)
            head(1)
            with pe.Fori(2, HEADS) as h:
                head(h)
            head(HEADS, own=False)

            with pe.Fori(0, 2) as k:
                for i in range(2):
                    full_block(2 * k + (N_GATE_B + 4 + i), i, h_hi, h_lo, free=(gb_scaled, 2 * k + (3 + i)))

            pe.wait_ge(rms_ready, 1)
            pe.wait_ge(ove_ready, HEADS)
            for t in range(NSC):
                last = nc.tensor.matmul(ps_a[:, t:t + 1], supers(inv_rms[:])[:, t, :], ident[:, 0:1],
                                        start=True, stop=True)
            last.then_inc(rms_turned, 1)

            def yb_pair(k):
                for i in range(2):
                    def wait_o(c):
                        pe.wait_ge(o_hi_ready, c + 1)
                        pe.wait_ge(o_lo_ready, c + 1)
                    full_block(2 * k + (N_OUT_B + i), i, o_hi, o_lo,
                               free=(part_ready, 2 * k + (i - 1)) if later(k) else (gb_scaled, KC - 1 + i),
                               wait_chunk=None if later(k) or i else wait_o)
            stepped(pe, KC // 2, yb_pair)

            for f in range(2):
                for b in range(4):
                    i = b % 2
                    wait_block(N_V + 4 * f + b)
                    wide_hi, wide_lo = (w[i][:].rearrange("p (kk g) n -> p kk (g n)", kk=2) for w in (w_hi, w_lo))
                    for kk in range(2):
                        k = 2 * b + kk
                        for t in range(NSC):
                            if k == 0:
                                if f:
                                    pe.wait_ge(v_tok_ready, t + 1)
                                elif t == 0:
                                    pe.wait_ge(part_ready, KC - 1)
                                elif t == 2:
                                    pe.wait_ge(part_ready, KC)
                                elif t == 4:
                                    pe.wait_ge(rms_tok_ready, 1)
                                elif t == 6:
                                    pe.wait_ge(ob_ready, HEADS)
                            s = slice(P * t, P * t + P)
                            nc.tensor.matmul(v_bank(t), h_hi[:, k, s], wide_hi[:, kk, :], start=(k == 0), stop=False)
                            nc.tensor.matmul(v_bank(t), h_lo[:, k, s], wide_hi[:, kk, :], start=False, stop=False)
                            last = nc.tensor.matmul(v_bank(t), h_hi[:, k, s], wide_lo[:, kk, :],
                                                    start=False, stop=(k == KC - 1))
                            if k == KC - 1 and t < NSC - 1:
                                last.then_inc(v_done, 1)
                    last.then_inc(proj_done, 2)

            def row_sums():
                pe.wait_ge(const_ready, 4)
                pe.wait_ge(v_tok_ready, 2 * NSC)
                for half in range(2):
                    last = nc.tensor.matmul(ps_b[:, halves[half]], ones[:],
                                            spatial_t[:, 4 * half:4 * half + 4, :].rearrange("p g t -> p (g t)"),
                                            start=True, stop=True)
                last.then_inc(rowsum_done, 1)

            def mixing(g, i):
                pe.wait_ge(z_ready, g + 1)
                if later(g):
                    pe.wait_ge(mix_ready, g)
                else:
                    pe.wait_ge(v_tok_ready, 2 * NSC)
                ps = [ps_a, ps_b][i]
                for c in range(NSC):
                    rhs = spatial_t[:, g, :]
                    last = nc.tensor.matmul(supers(ps[:])[:, c, :], supers(work[2][:])[:, c, :], rhs,
                                            start=True, stop=True)
                last.then_inc(mixed_done, 1)

            def u_pair(k):
                for i in range(2):
                    n = 2 * k + (N_U + i)
                    free = (u_scaled, 2 * k + (i - 1)) if later(k) else (v_tok_ready, NSC + 2 + 2 * i)
                    half_block(n, i, 0, h_hi, h_lo, free=free,
                               between=None if i or later(k) else (4, row_sums))
                    if i or later(k):
                        mixing(2 * k + (i - 1), 1 - i)
                    half_block(n, i, 1, h_hi, h_lo)
            stepped(pe, KC // 2, u_pair)

            def a_step(j):
                n = 2 * j + N_GATE_A
                half_block(n, 0, 0, h_hi, h_lo, free=(ga_scaled, j) if later(j) else (u_scaled, KC - 1))
                if not later(j):
                    mixing(KC - 1, 1)
                half_block(n, 0, 1, h_hi, h_lo)

                def wait_a(c):
                    pe.wait_ge(a_hi_ready, c + 1)
                    pe.wait_ge(a_lo_ready, c + 1)
                full_block(n + 1, 1, a_hi, a_lo, free=(ya_ready, j) if later(j) else (u_scaled, KC),
                           wait_chunk=None if later(j) else wait_a)
            stepped(pe, KC, a_step)

            def out_pair(k):
                for i in range(2):
                    def wait_m(c):
                        pe.wait_ge(m_hi_ready, c + 1)
                        pe.wait_ge(m_lo_ready, c + 1)
                    if later(k):
                        free = (x1_ready, 2 * k + (i - 1))
                    else:
                        free = [(ga_scaled, KC), (ya_ready, KC)][i]
                    full_block(2 * k + (N_MERGE + i), i, h_hi, merged_lo, free=free,
                               wait_chunk=None if later(k) or i else wait_m)
            stepped(pe, KC // 2, out_pair)

            def wait_ffn(c):
                pe.wait_ge(ffn_hi_ready, c + 1)
                pe.wait_ge(ffn_lo_ready, c + 1)

            for p, parts in enumerate(PARTS):
                def ff_step(j):
                    n = N_PART[p] + 2 * j
                    k = act_before[p] + j
                    if later(j):
                        free_gate, free_up = (ff_scaled, k), (act_raw, k)
                    elif p == 0:
                        free_gate, free_up = (x1_ready, KC - 1), (x1_ready, KC)
                    else:
                        free_gate, free_up = (down_ready, KC * p - 1), (down_ready, KC * p)
                    if p == 0 and not later(j):
                        full_block(n, 0, ffn_hi, h_lo, free=free_gate, wait_chunk=wait_ffn)
                        sum_squares(work[0], ssq_step, KC)
                    else:
                        full_block(n, 0, ffn_hi, h_lo, free=free_gate)
                    full_block(n + 1, 1, ffn_hi, h_lo, free=free_up)
                stepped(pe, parts, ff_step)
                n_down = N_PART[p] + 2 * parts
                done = act_before[p] + parts
                if p == len(PARTS) - 1:
                    continue

                def wait_act(c):
                    pe.wait_ge(act_hi_ready, act_before[p] + c + 1)
                    pe.wait_ge(act_lo_ready, act_before[p] + c + 1)

                def down_pair(k):
                    for i in range(2):
                        if later(k):
                            free = (down_ready, 2 * k + (KC * p + i - 1))
                        else:
                            free = [(ff_scaled, done), (act_raw, done)][i]
                        full_block(2 * k + (n_down + i), i, act_hi, act_lo, free=free, chunks_in=parts,
                                   wait_chunk=None if later(k) or i else wait_act)
                stepped(pe, KC // 2, down_pair)

            for part, s in enumerate(tail_tokens):
                for c in range(KC):
                    q = KC * part + c
                    if part == 0:
                        pe.wait_ge(w_hi_ready, n_tail + c + 1)
                        pe.wait_ge(w_lo_ready, n_tail + c + 1)
                    if q >= 4:
                        pe.wait_ge(down_ready, KC * (len(PARTS) - 1) + q - 3)
                    elif q == 0:
                        pe.wait_ge(ff_scaled, FC)
                    elif q == 2:
                        pe.wait_ge(act_raw, FC)
                    hi, lo = tail_weight(c)
                    out = tail_bank(q, s)
                    for k in range(last_parts):
                        if q == 0:
                            pe.wait_ge(act_hi_ready, FC - last_parts + k + 1)
                            pe.wait_ge(act_lo_ready, FC - last_parts + k + 1)
                        nc.tensor.matmul(out, hi[:, k, :], act_hi[:, k, s], start=(k == 0), stop=False)
                        nc.tensor.matmul(out, hi[:, k, :], act_lo[:, k, s], start=False, stop=False)
                        last = nc.tensor.matmul(out, lo[:, k, :], act_hi[:, k, s], start=False,
                                                stop=(k == last_parts - 1))
                    last.then_inc(tail_done, 1)
                    if part and c == 1:
                        tail_squares(part - 1)
            tail_squares(len(tail_tokens) - 1)


def kernel(x, norm_mix_g, w_in, gmlp_ln_g, gmlp_ln_b, gmlp_w_s, gmlp_b_s, hgrn_lb_table, hgrn_norm_g,
           w_branch_a, w_branch_b, w_out, norm_ffn_g, w_gate_up, w_down, norm_final_g):
    import numpy as np
    import concourse.bacc as bacc
    from concourse.bass_utils import run_bass_kernel_spmd

    def blocks(w):
        w = np.asarray(w)
        return w.reshape(w.shape[0] // P, P, w.shape[1] // P, P).transpose(2, 1, 0, 3)

    x = np.asarray(x)
    w_in_b = blocks(np.asarray(w_in)[0])
    u, v, q, f, i, g, ga, gb = (w_in_b[KC * k:KC * k + KC] for k in range(8))
    wa, wb, wo = (blocks(np.asarray(w)[0]) for w in (w_branch_a, w_branch_b, w_out))
    gu, dn = blocks(np.asarray(w_gate_up)[0]), blocks(np.asarray(w_down)[0])
    stream = np.zeros((N_BLOCKS, P, KC, P), np.float32)
    for head in range(HEADS):
        for b, w in enumerate((f, q, i, g)):
            stream[N_HEAD + 4 * head + b] = w[head]
    for c in range(KC):
        stream[N_GATE_B + c] = gb[c]
        stream[N_OUT_B + c] = wb[c]
        wide, b = divmod(c, 4)
        stream[N_V + c] = v[4 * wide:4 * wide + 4, :, 2 * b:2 * b + 2].transpose(1, 2, 0, 3).reshape(P, KC, P)
        stream[N_U + c] = u[c]
        stream[N_GATE_A + 2 * c] = ga[c]
        stream[N_GATE_A + 2 * c + 1] = wa[c]
        stream[N_MERGE + c] = wo[c]
    at = 0
    for p, parts in enumerate(PARTS):
        for j in range(parts):
            stream[N_PART[p] + 2 * j] = gu[at + j]
            stream[N_PART[p] + 2 * j + 1] = gu[FC + at + j]
        for c in range(KC):
            stream[N_PART[p] + 2 * parts + c, :, :parts] = dn[c][:, at:at + parts]
        at += parts
    per_feature = [np.asarray(norm_mix_g)[0], np.asarray(hgrn_lb_table)[0], np.asarray(hgrn_lb_table)[1],
                   np.asarray(hgrn_norm_g)[0], np.asarray(gmlp_ln_g)[0], np.asarray(gmlp_ln_b)[0],
                   np.asarray(norm_ffn_g)[0], np.asarray(norm_final_g)]
    arrays = {
        "x_t": np.ascontiguousarray(x[0].T.reshape(KC, P, T).transpose(1, 0, 2)),
        "w_stream": stream,
        "vectors": np.ascontiguousarray(np.stack([a.reshape(KC, P).T for a in per_feature], axis=1)),
        "w_spatial": np.ascontiguousarray(np.asarray(gmlp_w_s)[0].transpose(2, 0, 1)),
        "b_spatial": np.ascontiguousarray(np.asarray(gmlp_b_s)[0].reshape(1, KC * P)),
    }
    nc = bacc.Bacc("TRN2", target_bir_lowering=False, num_devices=1)
    args = [nc.dram_tensor(name, a.shape, F32, kind="ExternalInput").ap() for name, a in arrays.items()]
    out_t = nc.dram_tensor("out_t", (P, KC, T), F32, kind="ExternalOutput").ap()
    build(nc, *args, out_t)
    r = run_bass_kernel_spmd(nc, [arrays], core_ids=[0])
    out = np.asarray(r.results[0]["out_t"])
    return np.ascontiguousarray(out.transpose(1, 0, 2).reshape(D, T).T.reshape(1, T, D))
```
